# Optimizing a Trainium2 kernel written in Bass

```python
import math
import jax, jax.numpy as jnp
from jax import lax
import numpy as np

D_MODEL = 1024
BATCH = 1
SEQ = 256
DEPTH = 2

N_MIXERS = 2
N_RG_LAYERS = (DEPTH + 1) // 2
N_AT_LAYERS = DEPTH // 2
NORM_EPS = 1e-6

LRU_WIDTH = D_MODEL
LRU_N_BLOCKS = 4
LRU_BLOCK_W = LRU_WIDTH // LRU_N_BLOCKS
CONV_WIDTH = 4
LRU_C = 8.0
A_MIN, A_MAX = 0.9, 0.999

ATT_WIDTH = D_MODEL
N_HEADS = 8
HEAD_DIM = ATT_WIDTH // N_HEADS
ROT_DIM = HEAD_DIM // 4
ROPE_THETA = 500000.0
MOBA_BLOCK = 256
MOBA_TOPK = 3
Q_CHUNK = 16

kernel_name = "hybrid_rglru_moba_gated"

def rms_norm(x, g):
    xf = x.astype(jnp.float32)
    y = xf * lax.rsqrt(jnp.mean(xf * xf, axis=-1, keepdims=True) + NORM_EPS)
    return (y * g.astype(jnp.float32)).astype(x.dtype)

def causal_depthwise_conv(x, w, b):
    width = x.shape[-1]
    y = lax.conv_general_dilated(
        x, w[:, None, :].astype(x.dtype), window_strides=(1,),
        padding=[(CONV_WIDTH - 1, 0)], dimension_numbers=("NWC", "WIO", "NWC"),
        feature_group_count=width)
    return y + b.astype(x.dtype)

def block_diag_linear(x, w, b):
    bsz, s, _ = x.shape
    xb = x.reshape(bsz, s, LRU_N_BLOCKS, LRU_BLOCK_W)
    y = jnp.einsum("bsnd,nde->bsne", xb, w.astype(x.dtype)) + b.astype(x.dtype)
    return y.reshape(bsz, s, LRU_WIDTH)

def _linear_scan_op(c1, c2):
    a1, b1 = c1
    a2, b2 = c2
    return a1 * a2, a2 * b1 + b2

def rg_lru(x, w_r, b_r, w_i, b_i, lam):
    r = jax.nn.sigmoid(block_diag_linear(x, w_r, b_r).astype(jnp.float32))
    i = jax.nn.sigmoid(block_diag_linear(x, w_i, b_i).astype(jnp.float32))
    log_a = LRU_C * r * jax.nn.log_sigmoid(lam.astype(jnp.float32))
    a = jnp.exp(log_a)
    mult = jnp.sqrt(jnp.maximum(1.0 - jnp.exp(2.0 * log_a), 0.0))
    u = mult * (i * x.astype(jnp.float32))
    _, h = lax.associative_scan(_linear_scan_op, (a, u), axis=1)
    return h.astype(x.dtype)

def recurrent_mixer(h, w_in, conv_w, conv_b, w_r, b_r, w_i, b_i, lam, w_out):
    proj = h @ w_in.astype(h.dtype)
    xb, gate = proj[..., :LRU_WIDTH], proj[..., LRU_WIDTH:]
    xb = causal_depthwise_conv(xb, conv_w, conv_b)
    y = rg_lru(xb, w_r, b_r, w_i, b_i, lam)
    return (y * jax.nn.silu(gate)) @ w_out.astype(h.dtype)

def rotary_tables(s):
    pos = jnp.arange(s, dtype=jnp.float32)
    inv_freq = ROPE_THETA ** (-jnp.arange(0, ROT_DIM, 2, dtype=jnp.float32) / ROT_DIM)
    ang = pos[:, None] * inv_freq[None, :]
    return jnp.cos(ang), jnp.sin(ang)

def apply_partial_rotary(x, cos, sin):
    half = ROT_DIM // 2
    x1, x2, xp = x[..., :half], x[..., half:ROT_DIM], x[..., ROT_DIM:]
    c, s = cos.astype(x.dtype), sin.astype(x.dtype)
    return jnp.concatenate([x1 * c - x2 * s, x2 * c + x1 * s, xp], axis=-1)

def moba_attention(q, k, v):
    bsz, nh, s, hd = q.shape
    scale = 1.0 / math.sqrt(hd)
    n_blk = -(-s // MOBA_BLOCK)
    pad = n_blk * MOBA_BLOCK - s
    k_p = jnp.pad(k, ((0, 0), (0, 0), (0, pad), (0, 0)))
    v_p = jnp.pad(v, ((0, 0), (0, 0), (0, pad), (0, 0)))
    k_blocks = k_p.reshape(bsz, nh, n_blk, MOBA_BLOCK, hd)
    v_blocks = v_p.reshape(bsz, nh, n_blk, MOBA_BLOCK, hd)

    k_mean = jnp.mean(k_blocks.astype(jnp.float32), axis=3)
    pos = jnp.arange(s)
    q_blk = pos // MOBA_BLOCK
    gate = jnp.einsum("bhsd,bhnd->bhsn", q.astype(jnp.float32), k_mean)
    past = jnp.arange(n_blk)[None, :] < q_blk[:, None]
    gate = jnp.where(past[None, None], gate, -jnp.inf)
    k_top = min(MOBA_TOPK, n_blk)
    _, sel = lax.top_k(gate, k_top)
    slot_valid = jnp.arange(k_top)[None, :] < q_blk[:, None]

    b_idx = jnp.arange(bsz)[:, None, None, None]
    h_idx = jnp.arange(nh)[None, :, None, None]
    n_chunks = s // Q_CHUNK

    def chunk(c):
        start = c * Q_CHUNK
        qc = lax.dynamic_slice_in_dim(q, start, Q_CHUNK, axis=2)
        sel_c = lax.dynamic_slice_in_dim(sel, start, Q_CHUNK, axis=2)
        valid_c = lax.dynamic_slice_in_dim(slot_valid, start, Q_CHUNK, axis=0)
        qpos = start + jnp.arange(Q_CHUNK)
        blk = start // MOBA_BLOCK
        own_k = lax.dynamic_slice_in_dim(k_p, blk * MOBA_BLOCK, MOBA_BLOCK, axis=2)
        own_v = lax.dynamic_slice_in_dim(v_p, blk * MOBA_BLOCK, MOBA_BLOCK, axis=2)
        k_sel = k_blocks[b_idx, h_idx, sel_c]
        v_sel = v_blocks[b_idx, h_idx, sel_c]
        s_sel = jnp.einsum("bhqd,bhqnkd->bhqnk", qc, k_sel).astype(jnp.float32) * scale
        s_sel = jnp.where(valid_c[None, None, :, :, None], s_sel, -jnp.inf)
        s_own = jnp.einsum("bhqd,bhkd->bhqk", qc, own_k).astype(jnp.float32) * scale
        key_pos = blk * MOBA_BLOCK + jnp.arange(MOBA_BLOCK)
        s_own = jnp.where((key_pos[None, :] <= qpos[:, None])[None, None], s_own, -jnp.inf)
        logits = jnp.concatenate(
            [s_sel.reshape(bsz, nh, Q_CHUNK, k_top * MOBA_BLOCK), s_own], axis=-1)
        p = jax.nn.softmax(logits, axis=-1).astype(v.dtype)
        p_sel = p[..., :k_top * MOBA_BLOCK].reshape(bsz, nh, Q_CHUNK, k_top, MOBA_BLOCK)
        p_own = p[..., k_top * MOBA_BLOCK:]
        return (jnp.einsum("bhqnk,bhqnkd->bhqd", p_sel, v_sel)
                + jnp.einsum("bhqk,bhkd->bhqd", p_own, own_v))

    out = lax.map(chunk, jnp.arange(n_chunks))
    return jnp.transpose(out, (1, 2, 0, 3, 4)).reshape(bsz, nh, s, hd)

def attention_mixer(h, w_in, w_out, cos, sin):
    bsz, s, _ = h.shape
    proj = h @ w_in.astype(h.dtype)
    q, k, v, gate = jnp.split(proj, 4, axis=-1)

    def heads(t):
        return t.reshape(bsz, s, N_HEADS, HEAD_DIM).transpose(0, 2, 1, 3)

    q = apply_partial_rotary(heads(q), cos, sin)
    k = apply_partial_rotary(heads(k), cos, sin)
    o = moba_attention(q, k, heads(v))
    o = o.transpose(0, 2, 1, 3).reshape(bsz, s, ATT_WIDTH)
    return (o * jax.nn.silu(gate)) @ w_out.astype(h.dtype)

def setup_inputs(seed: int = 0) -> dict:
    key = jax.random.key(seed)
    ks = jax.random.split(key, 20)
    na, nb = N_RG_LAYERS, N_AT_LAYERS
    f32 = jnp.float32

    def nrm(k, shape, fan_in):
        return jax.random.normal(k, shape, f32) * (fan_in ** -0.5)

    a_c = jax.random.uniform(ks[9], (na, LRU_WIDTH), f32, A_MIN, A_MAX)
    a0 = a_c ** (1.0 / LRU_C)
    lam = jnp.log(a0) - jnp.log1p(-a0)
    return {
        "x": jax.random.normal(ks[0], (BATCH, SEQ, D_MODEL), f32),
        "rg_norm": 1.0 + 0.02 * jax.random.normal(ks[1], (na, D_MODEL), f32),
        "rg_w_in": nrm(ks[2], (na, D_MODEL, 2 * LRU_WIDTH), D_MODEL),
        "rg_conv_w": nrm(ks[3], (na, CONV_WIDTH, LRU_WIDTH), CONV_WIDTH),
        "rg_conv_b": 0.01 * jax.random.normal(ks[4], (na, LRU_WIDTH), f32),
        "rg_w_rgate": nrm(ks[5], (na, LRU_N_BLOCKS, LRU_BLOCK_W, LRU_BLOCK_W), LRU_BLOCK_W),
        "rg_b_rgate": 0.01 * jax.random.normal(ks[6], (na, LRU_N_BLOCKS, LRU_BLOCK_W), f32),
        "rg_w_igate": nrm(ks[7], (na, LRU_N_BLOCKS, LRU_BLOCK_W, LRU_BLOCK_W), LRU_BLOCK_W),
        "rg_b_igate": 0.01 * jax.random.normal(ks[8], (na, LRU_N_BLOCKS, LRU_BLOCK_W), f32),
        "rg_lambda": lam,
        "rg_w_out": nrm(ks[10], (na, LRU_WIDTH, D_MODEL), LRU_WIDTH),
        "at_norm": 1.0 + 0.02 * jax.random.normal(ks[11], (nb, D_MODEL), f32),
        "at_w_in": nrm(ks[12], (nb, D_MODEL, 4 * ATT_WIDTH), D_MODEL),
        "at_w_out": nrm(ks[13], (nb, ATT_WIDTH, D_MODEL), ATT_WIDTH),
        "final_norm": 1.0 + 0.02 * jax.random.normal(ks[14], (D_MODEL,), f32),
    }

def reference(x, rg_norm, rg_w_in, rg_conv_w, rg_conv_b, rg_w_rgate, rg_b_rgate,
              rg_w_igate, rg_b_igate, rg_lambda, rg_w_out, at_norm, at_w_in, at_w_out,
              final_norm):
    cos, sin = rotary_tables(x.shape[1])
    for i in range(DEPTH):
        j = i // N_MIXERS
        if i % N_MIXERS == 0:
            h = rms_norm(x, rg_norm[j])
            x = x + recurrent_mixer(h, rg_w_in[j], rg_conv_w[j], rg_conv_b[j],
                                    rg_w_rgate[j], rg_b_rgate[j], rg_w_igate[j],
                                    rg_b_igate[j], rg_lambda[j], rg_w_out[j])
        else:
            h = rms_norm(x, at_norm[j])
            x = x + attention_mixer(h, at_w_in[j], at_w_out[j], cos, sin)
    return rms_norm(x, final_norm)


_drawn_inputs = setup_inputs


def setup_inputs(seed=0):
    import zlib

    import numpy as np

    out = dict(_drawn_inputs(seed))
    spreads = {}
    factors = {'rg_norm': 6.063,
     'rg_b_rgate': 8.0,
     'rg_b_igate': 8.0,
     'at_norm': 8.0,
     'final_norm': 2.879}
    for name, (base, spread) in spreads.items():
        noise = np.random.default_rng([zlib.crc32(name.encode()), seed]).standard_normal(out[name].shape)
        drawn = base * np.exp(spread * noise) if base else spread * noise
        out[name] = __import__('jax').numpy.asarray(drawn.astype(out[name].dtype))
    for name, factor in factors.items():
        out[name] = (out[name] * factor).astype(out[name].dtype)
    return out
```

```python
from contextlib import ExitStack

import numpy as np

import concourse.bass as bass
from concourse import mybir
from concourse.alu_op_type import AluOpType as ALU

D = 1024
T = 256
P = 128
KT = D // P
TT = T // P
NR = 4
CW = D // NR
HT = CW // P
TAPS = 4
ROT = 32
HALF = ROT // 2
EPS = 1e-6
SCALE = float(P) ** -0.5
NCONST = TAPS + 4
CHUNK = KT * CW
GCHUNK = HT * 2 * CW

S_XQ, S_GK, S_RV, S_OG, S_O2 = range(5)
NSLOT = 5

F32, F32R, BF16 = mybir.dt.float32, mybir.dt.float32r, mybir.dt.bfloat16
ACT = mybir.ActivationFunctionType
AX = mybir.AxisListType.X


def build(nc, x_t, w_xq, w_gk, w_ri, w_v, w_og, w_o2, consts, gains, rope, ident_mask, out_t):
    ctx = ExitStack()
    with ctx:
        def sb(name, cols, dt=F32):
            return ctx.enter_context(nc.sbuf_tensor(name, [P, cols], dt))

        def sem(name):
            return ctx.enter_context(nc.semaphore(name))

        raw = [sb(f"raw{j}", CHUNK) for j in range(NSLOT)]
        whi = [sb(f"whi{j}", CHUNK, F32R) for j in range(NSLOT)]
        wlo = [sb(f"wlo{j}", CHUNK, F32R) for j in range(NSLOT)]
        xt = sb("xt", KT * T)
        hhi, hlo = sb("hhi", KT * T, F32R), sb("hlo", KT * T, F32R)
        sq = sb("sq", KT * T)
        con = sb("con", NR * HT * NCONST)
        gn = sb("gn", 3 * KT)
        rp = sb("rp", 2 * TT * HALF)
        idm = sb("idm", 2 * P)
        ones = sb("ones", P)
        zeros = sb("zeros", 2 * T, BF16)
        eps = sb("eps", 1)
        half_b = sb("half_b", NR * HT * 2)
        lam = sb("lam", 6 * NR * HT)
        c4 = sb("c4", NR * HT * 2)
        std, rinv = sb("std", T), sb("rinv", T)
        rtok = sb("rtok", 3 * TT)
        junk = sb("junk", P)
        con_v, con_a = sb("con_v", HT * NCONST), sb("con_a", HT * NCONST)
        cb_a = sb("cb_a", HT * 4)
        xc = sb("xc", CW * HT)
        xchi, xclo = sb("xchi", HT * T, F32R), sb("xclo", HT * T, F32R)
        tr, ti, tg = sb("tr", HT * T), sb("ti", HT * T), sb("tg", HT * T)
        av, a2 = sb("av", HT * T), sb("a2", HT * T)
        mv, ix = sb("mv", HT * T), sb("ix", HT * T)
        uu, hh = sb("uu", HT * T), sb("hh", HT * T)
        sg, yy = sb("sg", HT * T), sb("yy", HT * T)
        yhi, ylo = sb("yhi", HT * T, F32R), sb("ylo", HT * T, F32R)
        qk = sb("qk", TT * 4 * P)
        rt = sb("rt", 4 * TT * 4 * HALF)
        vv = sb("vv", TT * CW)
        qT, kT = tr, ti
        gs = av
        pr = sb("pr", HT * 3 * P)
        pT = sb("pT", HT * 3 * P)
        mx, nb, rs, rc = (sb(n, HT * TT) for n in ("mx", "nb", "rs", "rc"))

        def psum(name):
            return ctx.enter_context(nc.psum_tensor(name, [P, 2 * T], F32))

        W = [psum(f"work{i}") for i in range(4)]
        A = [psum(f"acc{i}") for i in range(4)]

        def v3(t, n, m, at=0):
            return t[:, at:at + n * m].rearrange("p (n m) -> p n m", n=n)

        def f(t):
            return t.bitcast(F32)

        g_rg, g_at, g_fin = (gn[:, i * KT:(i + 1) * KT] for i in range(3))
        cos_t, sin_t = (rp[:, i * TT * HALF:(i + 1) * TT * HALF] for i in range(2))
        ident, mask = idm[:, 0:P], idm[:, P:2 * P]

        raw_in = [sem(f"raw_in{j}") for j in range(NSLOT)]
        hi_rdy = [sem(f"hi_rdy{j}") for j in range(NSLOT)]
        lo_rdy = [sem(f"lo_rdy{j}") for j in range(NSLOT)]
        used = [sem(f"used{j}") for j in range(NSLOT)]
        (x_in, c_in, i_in, const_rdy, sq_rdy, ss_done, std_rdy, rinv_rdy, h_hi, h_lo, lamS, c4_rdy, hb_rdy, e_lam,
         zero_done, con_v_rdy, con_a_rdy, r_done, out_done, xc_init, conv_step, xchi_rdy,
         xclo_rdy, tr_rdy, ti_rdy, tg_rdy, a_rdy, a2_rdy, a2c_rdy, m_rdy, ix_rdy, u_rdy, scan_rdy, sg_rdy, y_rdy,
         yhi_rdy, ylo_rdy, x1_rdy, rtok_rdy, q_rdy, k_rdy, v_rdy, rope_m, rope_rdy, t_done,
         qT_rdy, kT_rdy, gs_rdy, s_done, masked, mx_rdy, nb_rdy, exp_rdy, rc_rdy, pr_rdy, pT_done, pT_a,
         pT_v, o_done, out_w, out_rdy) = (sem(n) for n in (
             "x_in c_in i_in const_rdy sq_rdy ss_done std_rdy rinv_rdy h_hi h_lo lamS c4_rdy hb_rdy e_lam "
             "zero_done con_v_rdy con_a_rdy r_done out_done xc_init conv_step xchi_rdy "
             "xclo_rdy tr_rdy ti_rdy tg_rdy a_rdy a2_rdy a2c_rdy m_rdy ix_rdy u_rdy scan_rdy sg_rdy y_rdy "
             "yhi_rdy ylo_rdy x1_rdy rtok_rdy q_rdy k_rdy v_rdy rope_m rope_rdy t_done "
             "qT_rdy kT_rdy gs_rdy s_done masked mx_rdy nb_rdy exp_rdy rc_rdy pr_rdy pT_done pT_a "
             "pT_v o_done out_w out_rdy").split())

        block = ctx.enter_context(nc.Block())

        @block.sync
        def _(sp):
            def load(j, n, dram, at, words=CHUNK, first=False):
                if not first:
                    sp.wait_ge(hi_rdy[j], n)
                    sp.wait_ge(lo_rdy[j], n)
                sp.dma_start(raw[j][:, 0:words],
                             dram[bass.ds(at, 1), :, :].rearrange("a p c -> p (a c)")).then_inc(raw_in[j], 16)

            sp.dma_start(xt[:, :], x_t).then_inc(x_in, 16)
            load(S_XQ, 0, w_xq, 0, first=True)
            load(S_GK, 0, w_gk, 0, first=True)
            load(S_RV, 0, w_ri, 0, GCHUNK, first=True)
            load(S_OG, 0, w_og, 0, first=True)
            load(S_O2, 0, w_o2, 0, first=True)
            with sp.Fori(1, NR) as r:
                load(S_XQ, r, w_xq, r)
                load(S_GK, r, w_gk, r)
                load(S_RV, r, w_ri, r, GCHUNK)
                load(S_OG, r, w_og, r)
            with sp.Fori(0, NR) as r:
                load(S_XQ, r + NR, w_xq, r + NR)
                load(S_GK, r + NR, w_gk, r + NR)
                load(S_RV, r + NR, w_v, r)
                load(S_OG, r + NR, w_og, r + NR)
            with sp.Fori(1, NR) as r:
                load(S_O2, r, w_o2, r)
            for c in range(4):
                sp.wait_ge(out_rdy, c + 1)
                sp.dma_start(out_t[:, c * 2 * T:(c + 1) * 2 * T], sq[:, c * 2 * T:(c + 1) * 2 * T]).then_inc(out_w, 16)
            sp.wait_ge(out_w, 4 * 16)

        @block.gpsimd
        def _(pool):
            pool.dma_start(con[:, :], consts).then_inc(c_in, 16)
            pool.dma_start(gn[:, :], gains).then_inc(c_in, 16)
            pool.dma_start(rp[:, :], rope).then_inc(i_in, 16)
            pool.dma_start(idm[:, :], ident_mask).then_inc(i_in, 16)
            pool.memset(ones[:, :], 1.0).then_inc(const_rdy, 1)
            pool.memset(eps[:, :], EPS).then_inc(const_rdy, 1)
            pool.memset(zeros[:, :], 0.0).then_inc(const_rdy, 1)

        @block.tensor
        def _(pe):
            def mm(o, w, x, start=False, stop=False):
                return pe.matmul(o, w, x, start=start, stop=stop, skip_group_check=True)

            def split3(o, ahi, alo, bhi, blo, start, stop):
                mm(o, ahi, bhi, start=start)
                mm(o, ahi, blo)
                return mm(o, alo, bhi, stop=stop)

            def chunk_ready(j, n):
                pe.wait_ge(hi_rdy[j], n + 1)
                pe.wait_ge(lo_rdy[j], n + 1)

            def project(j, n, bank, wait_h=0):
                chunk_ready(j, n)
                for k in range(KT):
                    if wait_h:
                        pe.wait_ge(h_hi, (wait_h - 1) * KT + k + 1)
                        pe.wait_ge(h_lo, (wait_h - 1) * KT + k + 1)
                    for m in range(HT):
                        w = slice(k * CW + m * P, k * CW + m * P + P)
                        h = slice(k * T, (k + 1) * T)
                        last = split3(bank[:, m * T:(m + 1) * T], whi[j][:, w], wlo[j][:, w], hhi[:, h], hlo[:, h],
                                      k == 0 and m == 0, k == KT - 1)
                last.then_inc(used[j], 1)

            def project_tok(j, n, bank, wait_h=0):
                chunk_ready(j, n)
                for k in range(KT):
                    if wait_h:
                        pe.wait_ge(h_hi, (wait_h - 1) * KT + k + 1)
                        pe.wait_ge(h_lo, (wait_h - 1) * KT + k + 1)
                    for t in range(TT):
                        w = slice(k * CW, (k + 1) * CW)
                        h = slice(k * T + t * P, k * T + t * P + P)
                        last = split3(bank[:, t * CW:(t + 1) * CW], hhi[:, h], hlo[:, h], whi[j][:, w], wlo[j][:, w],
                                      k == 0 and t == 0, k == KT - 1)
                last.then_inc(used[j], 1)

            def clear_acc():
                for a in A:
                    last = mm(a[:, :], zeros[:, 0:P], zeros[:, :], start=True)
                last.then_inc(zero_done, 1)

            def project_out(j, n, yn, last_of_layer=False):
                chunk_ready(j, n)
                pe.wait_ge(yhi_rdy, yn + 1)
                pe.wait_ge(ylo_rdy, yn + 1)
                for c in range(KT):
                    for k in range(HT):
                        w = slice(k * D + c * P, k * D + c * P + P)
                        y = slice(k * T, (k + 1) * T)
                        last = split3(A[c // 2][:, (c % 2) * T:(c % 2 + 1) * T], whi[j][:, w], wlo[j][:, w],
                                      yhi[:, y], ylo[:, y], False, last_of_layer and k == HT - 1)
                    if last_of_layer and c % 2 == 1 and c < KT - 1:
                        last.then_inc(out_done, 1)
                last.then_inc(used[j], 1)

            def sum_squares(n):
                for k in range(KT):
                    if k % 2 == 0:
                        pe.wait_ge(sq_rdy, 4 * n + k // 2 + 1)
                    last = mm(W[1][:, 0:T], ones[:, :], sq[:, k * T:(k + 1) * T], start=k == 0, stop=k == KT - 1)
                last.then_inc(ss_done, 1)

            pe.wait_ge(const_rdy, 3)
            clear_acc()
            sum_squares(0)

            def round1(r, first=False):
                pe_gate_wait = not first
                if pe_gate_wait:
                    pe.wait_ge(conv_step, r * 6)
                project(S_XQ, r, W[0], wait_h=1 if first else 0)
                if first:
                    pe.wait_ge(std_rdy, 1)
                else:
                    pe.wait_ge(sg_rdy, r)
                project(S_GK, r, W[1])
                chunk_ready(S_RV, r)
                pe.wait_ge(xchi_rdy, r + 1)
                pe.wait_ge(xclo_rdy, r + 1)
                if not first:
                    pe.wait_ge(tr_rdy, r)
                    pe.wait_ge(ti_rdy, r)
                for g in range(2):
                    for m in range(HT):
                        for k in range(HT):
                            w = slice(k * 2 * CW + g * CW + m * P, k * 2 * CW + g * CW + m * P + P)
                            x = slice(k * T, (k + 1) * T)
                            last = split3(W[2 + g][:, m * T:(m + 1) * T], whi[S_RV][:, w], wlo[S_RV][:, w],
                                          xchi[:, x], xclo[:, x], m == 0 and k == 0, k == HT - 1)
                    last.then_inc(used[S_RV] if g else r_done, 1)
                if not first:
                    project_out(S_OG, r - 1, r - 1)

            round1(0, first=True)
            with pe.Fori(1, NR) as r:
                round1(r)
            project_out(S_OG, NR - 1, NR - 1, last_of_layer=True)

            def pv(r):
                pe.wait_ge(pT_a, r + 1)
                pe.wait_ge(pT_v, r + 1)
                for h in range(HT):
                    mm(W[1][:, h * T:(h + 1) * T], vv[:, h * P:(h + 1) * P], pT[:, h * 3 * P:h * 3 * P + T], start=True)
                    last = mm(W[1][:, h * T + P:(h + 1) * T], vv[:, CW + h * P:CW + (h + 1) * P],
                              pT[:, h * 3 * P + T:(h + 1) * 3 * P], stop=True)
                last.then_inc(o_done, 1)

            def round2(r, first=False):
                n = r + NR
                if not first:
                    pe.wait_ge(exp_rdy, 4 * r)
                else:
                    pe.wait_ge(conv_step, NR * 6)
                project_tok(S_XQ, n, W[0], wait_h=2 if first else 0)
                if first:
                    pe.wait_ge(sg_rdy, NR)
                    sum_squares(1)
                    clear_acc()
                    pe.wait_ge(tr_rdy, NR)
                    pe.wait_ge(ti_rdy, NR)
                else:
                    pv(r - 1)
                    pe.wait_ge(pT_v, r)
                project_tok(S_GK, n, W[2])
                if not first:
                    pe.wait_ge(masked, 2 * r)
                    pe.wait_ge(exp_rdy, 4 * r)
                project_tok(S_RV, n, W[3])
                pe.wait_ge(rope_rdy, r + 1)
                if not first:
                    pe.wait_ge(y_rdy, r + NR)
                for b, g0 in ((0, 0), (1, 2)):
                    for h in range(HT):
                        for t in range(TT):
                            last = pe.transpose(W[b][:, h * T + t * P:h * T + (t + 1) * P],
                                                qk[:, (t * 4 + g0 + h) * P:(t * 4 + g0 + h + 1) * P], ident)
                last.then_inc(t_done, 1)
                pe.wait_ge(k_rdy, r + 1)
                project(S_OG, n, W[2])
                pe.wait_ge(qT_rdy, r + 1)
                pe.wait_ge(kT_rdy, r + 1)
                pe.wait_ge(v_rdy, r + 1)
                for h, b in ((0, 3), (1, 0)):
                    mm(W[b][:, 0:P], qT[:, h * T:h * T + P], kT[:, h * T:h * T + P], start=True, stop=True)
                    mm(W[b][:, P:3 * P], qT[:, h * T + P:(h + 1) * T], kT[:, h * T:(h + 1) * T],
                       start=True, stop=True).then_inc(s_done, 1)
                if not first:
                    project_out(S_O2, r - 1, NR + r - 1)
                pe.wait_ge(gs_rdy, r + 1)
                for h in range(HT):
                    pe.wait_ge(pr_rdy, 4 * r + 2 * h + 2)
                    for i in range(3):
                        s = slice((h * 3 + i) * P, (h * 3 + i + 1) * P)
                        last = pe.transpose(W[1 + h][:, i * P:(i + 1) * P], pr[:, s], ident)
                    last.then_inc(pT_done, 1)

            pe.wait_ge(i_in, 32)
            round2(0, first=True)
            with pe.Fori(1, NR) as r:
                round2(r)
            pv(NR - 1)
            project_out(S_O2, NR - 1, 2 * NR - 1, last_of_layer=True)
            pe.wait_ge(y_rdy, 2 * NR)
            sum_squares(2)

        @block.scalar
        def _(act):
            def split_hi(j, n, words=CHUNK, slot_free=False):
                act.wait_ge(raw_in[j], 16 * n + 16)
                if not slot_free:
                    act.wait_ge(used[j], n)
                nc.scalar.activation(whi[j][:, 0:words], raw[j][:, 0:words], ACT.Copy).then_inc(hi_rdy[j], 1)

            act.wait_ge(x_in, 16)
            for c in range(4):
                s = slice(c * 2 * T, (c + 1) * 2 * T)
                nc.scalar.activation(sq[:, s], xt[:, s], ACT.Square).then_inc(sq_rdy, 1)
            act.wait_ge(ss_done, 1)
            act.wait_ge(const_rdy, 2)
            nc.scalar.activation(std[:, :], W[1][:, 0:T], ACT.Sqrt, bias=eps[:, :], scale=1.0 / D).then_inc(std_rdy, 1)
            split_hi(S_XQ, 0, slot_free=True)
            act.wait_ge(rinv_rdy, 1)
            for k in range(KT):
                act.wait_ge(x1_rdy, k + 1)
                nc.scalar.activation(hhi[:, k * T:(k + 1) * T], sq[:, k * T:(k + 1) * T], ACT.Copy).then_inc(h_hi, 1)
            split_hi(S_GK, 0, slot_free=True)
            act.wait_ge(lamS, 1)
            L8 = NR * HT
            nc.scalar.activation(lam[:, L8:2 * L8], lam[:, 0:L8], ACT.Exp, scale=-1.0).then_inc(e_lam, 1)
            act.wait_ge(c4_rdy, 1)
            act.wait_ge(hb_rdy, 1)

            def round1(r, first=False):
                split_hi(S_RV, r, GCHUNK, first)
                if not first:
                    act.wait_ge(a2_rdy, HT * r)
                rr = bass.ds(r, 1)
                nc.scalar.activation(con_a[:, :], v3(con, NR, HT * NCONST)[:, rr, :].rearrange("p a c -> p (a c)"),
                                     ACT.Copy).then_inc(con_a_rdy, 1)
                nc.scalar.activation(cb_a[:, 0:HT * 2], v3(half_b, NR, HT * 2)[:, rr, :].rearrange("p a c -> p (a c)"),
                                     ACT.Copy).then_inc(con_a_rdy, 1)
                nc.scalar.activation(cb_a[:, HT * 2:HT * 4], v3(c4, NR, HT * 2)[:, rr, :].rearrange("p a c -> p (a c)"),
                                     ACT.Copy).then_inc(con_a_rdy, 1)
                act.wait_ge(con_a_rdy, 3 * r + 3)
                act.wait_ge(used[S_XQ], r + 1)
                if not first:
                    act.wait_ge(ix_rdy, r)
                    act.wait_ge(xclo_rdy, r)
                for m in range(HT):
                    c0 = m * NCONST
                    nc.scalar.activation(xc[:, m * T:(m + 1) * T], W[0][:, m * T:(m + 1) * T], ACT.Identity,
                                         bias=con_a[:, c0 + TAPS:c0 + TAPS + 1],
                                         scale=con_a[:, c0 + TAPS - 1:c0 + TAPS]).then_inc(xc_init, 1)
                if not first:
                    split_hi(S_OG, r - 1, slot_free=True)
                act.wait_ge(conv_step, 6 * r + 6)
                if not first:
                    act.wait_ge(used[S_RV], r)
                nc.scalar.activation(xchi[:, :], xc[:, :], ACT.Copy).then_inc(xchi_rdy, 1)
                act.wait_ge(used[S_GK], r + 1)
                if not first:
                    act.wait_ge(sg_rdy, r)
                nc.scalar.activation(tg[:, :], W[1][:, :], ACT.Tanh, scale=0.5).then_inc(tg_rdy, 1)
                for g, (t, rdy) in enumerate(((tr, tr_rdy), (ti, ti_rdy))):
                    act.wait_ge(used[S_RV] if g else r_done, r + 1)
                    if g == 1 and not first:
                        act.wait_ge(ix_rdy, r)
                    if g == 0 and not first:
                        act.wait_ge(a2_rdy, HT * r)
                    for m in range(HT):
                        ins = nc.scalar.activation(t[:, m * T:(m + 1) * T], W[2 + g][:, m * T:(m + 1) * T], ACT.Tanh,
                                                   bias=cb_a[:, m * 2 + g:m * 2 + g + 1], scale=0.5)
                    ins.then_inc(rdy, 1)
                act.wait_ge(tr_rdy, r + 1)
                if not first:
                    act.wait_ge(scan_rdy, HT * r)
                    act.wait_ge(m_rdy, r)
                for i, (dst, rdy) in enumerate(((a2, a2_rdy), (av, a_rdy))):
                    for m in range(HT):
                        c = cb_a[:, HT * 2 + m * 2 + 1 - i:HT * 2 + m * 2 + 2 - i]
                        nc.scalar.activation(dst[:, m * T:(m + 1) * T], tr[:, m * T:(m + 1) * T], ACT.Exp,
                                             bias=c, scale=c).then_inc(rdy, 1)
                act.wait_ge(a2c_rdy, r + 1)
                if not first:
                    act.wait_ge(u_rdy, r)
                nc.scalar.activation(mv[:, :], a2[:, :], ACT.Sqrt, bias=1.0, scale=-1.0).then_inc(m_rdy, 1)
                split_hi(S_XQ, r + 1)
                act.wait_ge(y_rdy, r + 1)
                if not first:
                    act.wait_ge(used[S_OG], r)
                nc.scalar.activation(yhi[:, :], yy[:, :], ACT.Copy).then_inc(yhi_rdy, 1)
                split_hi(S_GK, r + 1)

            round1(0, first=True)
            with act.Fori(1, NR) as r:
                round1(r)
            split_hi(S_OG, NR - 1)

            for c in range(4):
                act.wait_ge(x1_rdy, KT + c + 1)
                act.wait_ge(used[S_GK], NR)
                for k in (2 * c, 2 * c + 1):
                    nc.scalar.activation(hhi[:, k * T:(k + 1) * T], xt[:, k * T:(k + 1) * T], ACT.Copy,
                                         scale=g_at[:, k:k + 1]).then_inc(h_hi, 1)
                s = slice(c * 2 * T, (c + 1) * 2 * T)
                nc.scalar.activation(sq[:, s], xt[:, s], ACT.Square).then_inc(sq_rdy, 1)
            act.wait_ge(rtok_rdy, 1)
            nc.scalar.activation(rtok[:, TT:2 * TT], rtok[:, 0:TT], ACT.Sqrt, bias=eps[:, :],
                                 scale=1.0 / D).then_inc(std_rdy, 1)
            nc.scalar.activation(std[:, :], W[1][:, 0:T], ACT.Sqrt, bias=eps[:, :], scale=1.0 / D).then_inc(std_rdy, 1)
            act.wait_ge(rtok_rdy, 2)

            def token_scaled(dst, bank, rdy):
                for t in range(TT):
                    ins = nc.scalar.activation(dst(t), bank[:, t * CW:(t + 1) * CW], ACT.Copy,
                                               scale=rtok[:, 2 * TT + t:2 * TT + t + 1])
                ins.then_inc(rdy, 1)

            def round2(r, first=False, last=False):
                n = r + NR
                split_hi(S_RV, n)
                act.wait_ge(used[S_XQ], n + 1)
                if not first:
                    act.wait_ge(t_done, r)
                token_scaled(lambda t: qk[:, t * 4 * P:t * 4 * P + CW], W[0], q_rdy)
                if not first:
                    act.wait_ge(y_rdy, n)
                    nc.scalar.activation(yhi[:, :], yy[:, :], ACT.Copy).then_inc(yhi_rdy, 1)
                split_hi(S_OG, n)
                act.wait_ge(used[S_GK], n + 1)
                token_scaled(lambda t: qk[:, t * 4 * P + CW:(t + 1) * 4 * P], W[2], k_rdy)
                if not first:
                    split_hi(S_O2, r - 1, slot_free=True)
                act.wait_ge(used[S_RV], n + 1)
                if not first:
                    act.wait_ge(o_done, r)
                token_scaled(lambda t: vv[:, t * CW:(t + 1) * CW], W[3], v_rdy)
                act.wait_ge(t_done, r + 1)
                if not first:
                    act.wait_ge(s_done, 2 * r)
                nc.scalar.activation(qT[:, :], W[0][:, :], ACT.Copy).then_inc(qT_rdy, 1)
                if not last:
                    split_hi(S_XQ, n + 1)
                act.wait_ge(gs_rdy, r + 1)
                nc.scalar.activation(tg[:, :], gs[:, :], ACT.Tanh, scale=0.5).then_inc(tg_rdy, 1)
                for h, b in ((0, 3), (1, 0)):
                    act.wait_ge(nb_rdy, 2 * r + h + 1)
                    if not first:
                        act.wait_ge(pT_done, 2 * r)
                        act.wait_ge(rc_rdy, 2 * r)
                    for t in range(TT):
                        s = slice(0, P) if t == 0 else slice(P, 3 * P)
                        nc.scalar.activation(pr[:, h * 3 * P + s.start:h * 3 * P + s.stop], W[b][:, s], ACT.Exp,
                                             bias=nb[:, h * TT + t:h * TT + t + 1], scale=SCALE,
                                             accum_out=rs[:, h * TT + t:h * TT + t + 1]).then_inc(exp_rdy, 1)
                if not last:
                    split_hi(S_GK, n + 1)
                act.wait_ge(pT_done, 2 * r + 1)
                if not first:
                    act.wait_ge(o_done, r)
                nc.scalar.activation(pT[:, 0:3 * P], W[1][:, 0:3 * P], ACT.Copy).then_inc(pT_a, 1)

            round2(0, first=True)
            with act.Fori(1, NR - 1) as r:
                round2(r)
            round2(NR - 1, last=True)
            split_hi(S_O2, NR - 1)
            act.wait_ge(y_rdy, 2 * NR)
            nc.scalar.activation(yhi[:, :], yy[:, :], ACT.Copy).then_inc(yhi_rdy, 1)

            for c in range(4):
                act.wait_ge(x1_rdy, KT + 4 + c + 1)
                s = slice(c * 2 * T, (c + 1) * 2 * T)
                nc.scalar.activation(sq[:, s], xt[:, s], ACT.Square).then_inc(sq_rdy, 1)
            act.wait_ge(ss_done, 3)
            nc.scalar.activation(std[:, :], W[1][:, 0:T], ACT.Sqrt, bias=eps[:, :], scale=1.0 / D).then_inc(std_rdy, 1)

        @block.vector
        def _(dve):
            tt, stt, ts = nc.vector.tensor_tensor, nc.vector.scalar_tensor_tensor, nc.vector.tensor_scalar

            def split_lo(j, n, words=CHUNK):
                dve.wait_ge(hi_rdy[j], n + 1)
                tt(wlo[j][:, 0:words], raw[j][:, 0:words], f(whi[j])[:, 0:words], ALU.subtract)\
                    .then_inc(lo_rdy[j], 1)

            L8 = NR * HT
            con3 = v3(con, L8, NCONST)
            dve.wait_ge(c_in, 32)
            lam_in = con3[:, :, NCONST - 1]
            ts(v3(half_b, L8, 2), con3[:, :, TAPS + 1:TAPS + 3], 0.5, None, ALU.mult).then_inc(hb_rdy, 1)
            step = [1]

            def chain(ins):
                step[0] += 1
                ins.then_inc(lamS, 1)
                dve.wait_ge(lamS, step[0] - 1 + 0)

            L = [lam[:, i * L8:(i + 1) * L8] for i in range(6)]
            step[0] = 1
            ts(L[2], lam_in, -1.0, None, ALU.mult).then_inc(rope_m, 1)
            dve.wait_ge(rope_m, 1)
            tt(L[0], L[2], lam_in, ALU.max).then_inc(lamS, 1)
            dve.wait_ge(std_rdy, 1)
            nc.vector.reciprocal(rinv[:, :], std[:, :]).then_inc(rinv_rdy, 1)
            dve.wait_ge(rinv_rdy, 1)
            for k in range(KT):
                s = slice(k * T, (k + 1) * T)
                stt(sq[:, s], xt[:, s], g_rg[:, k:k + 1], rinv[:, :], ALU.mult, ALU.mult).then_inc(x1_rdy, 1)
            for k in range(KT):
                s = slice(k * T, (k + 1) * T)
                dve.wait_ge(h_hi, k + 1)
                tt(hlo[:, s], sq[:, s], f(hhi)[:, s], ALU.subtract).then_inc(h_lo, 1)
                if k == 1:
                    split_lo(S_XQ, 0)
            split_lo(S_GK, 0)
            dve.wait_ge(e_lam, 1)
            e = L[1]
            chain(ts(L[2], e, 2.0, None, ALU.add))
            dve.wait_ge(lamS, 2)
            chain(nc.vector.reciprocal(L[3], L[2]))
            dve.wait_ge(lamS, 3)
            chain(tt(L[2], e, L[3], ALU.mult))
            dve.wait_ge(lamS, 4)
            chain(tt(L[3], L[2], L[2], ALU.mult))
            dve.wait_ge(lamS, 5)
            NT = 8
            chain(ts(L[4], L[3], 1.0 / (2 * NT + 1), None, ALU.mult))
            count = 6
            for i in range(NT - 1, 0, -1):
                dve.wait_ge(lamS, count)
                chain(stt(L[4], L[4], 1.0 / (2 * i + 1), L[3], ALU.add, ALU.mult))
                count += 1
            dve.wait_ge(lamS, count)
            chain(stt(L[4], L[4], 1.0, L[2], ALU.add, ALU.mult))
            chain(ts(L[5], lam_in, 0.0, None, ALU.min))
            dve.wait_ge(lamS, count + 2)
            chain(stt(L[4], L[4], -2.0, L[5], ALU.mult, ALU.add))
            dve.wait_ge(lamS, count + 3)
            c43 = v3(c4, L8, 2)
            ts(c43[:, :, 0], L[4], 4.0, None, ALU.mult).then_inc(lamS, 1)
            ts(c43[:, :, 1], L[4], 8.0, None, ALU.mult).then_inc(lamS, 1)
            dve.wait_ge(lamS, count + 5)
            dve.sem_inc(c4_rdy, 1)

            def round1(r, first=False):
                split_lo(S_RV, r, GCHUNK)
                nc.vector.tensor_copy(con_v[:, :], v3(con, NR, HT * NCONST)[:, bass.ds(r, 1), :]
                                      .rearrange("p a c -> p (a c)")).then_inc(con_v_rdy, 1)
                dve.wait_ge(con_v_rdy, r + 1)
                for i in range(1, TAPS):
                    for m in range(HT):
                        dve.wait_ge(xc_init, HT * r + HT)
                        if i > 1:
                            dve.wait_ge(conv_step, 6 * r + (i - 2) * HT + m + 1)
                        c = m * NCONST + TAPS - 1 - i
                        o = xc[:, m * T + i:(m + 1) * T]
                        stt(o, W[0][:, m * T:(m + 1) * T - i], con_v[:, c:c + 1], o, ALU.mult, ALU.add)\
                            .then_inc(conv_step, 1)
                dve.wait_ge(xchi_rdy, r + 1)
                tt(xclo[:, :], xc[:, :], f(xchi)[:, :], ALU.subtract).then_inc(xclo_rdy, 1)
                if not first:
                    split_lo(S_OG, r - 1)
                dve.wait_ge(tg_rdy, r + 1)
                stt(sg[:, :], tg[:, :], 1.0, W[1][:, :], ALU.add, ALU.mult).then_inc(sg_rdy, 1)
                dve.wait_ge(ti_rdy, r + 1)
                stt(ix[:, :], ti[:, :], 1.0, xc[:, :], ALU.add, ALU.mult).then_inc(ix_rdy, 1)
                dve.wait_ge(a2_rdy, HT * (r + 1))
                ts(a2[:, :], a2[:, :], 1.0, None, ALU.min).then_inc(a2c_rdy, 1)
                split_lo(S_XQ, r + 1)
                dve.wait_ge(m_rdy, r + 1)
                dve.wait_ge(ix_rdy, r + 1)
                stt(uu[:, :], mv[:, :], 0.5, ix[:, :], ALU.mult, ALU.mult).then_inc(u_rdy, 1)
                dve.wait_ge(u_rdy, r + 1)
                dve.wait_ge(a_rdy, HT * (r + 1))
                for m in range(HT):
                    s = slice(m * T, (m + 1) * T)
                    nc.vector.tensor_tensor_scan(hh[:, s], av[:, s], uu[:, s], 0.0, ALU.mult, ALU.add)\
                        .then_inc(scan_rdy, 1)
                dve.wait_ge(scan_rdy, HT * (r + 1))
                dve.wait_ge(sg_rdy, r + 1)
                stt(yy[:, :], hh[:, :], 0.5, sg[:, :], ALU.mult, ALU.mult).then_inc(y_rdy, 1)
                dve.wait_ge(yhi_rdy, r + 1)
                tt(ylo[:, :], yy[:, :], f(yhi)[:, :], ALU.subtract).then_inc(ylo_rdy, 1)
                split_lo(S_GK, r + 1)

            round1(0, first=True)
            with dve.Fori(1, NR) as r:
                round1(r)
            split_lo(S_OG, NR - 1)

            def residual(c, n):
                if c < 3:
                    dve.wait_ge(out_done, 3 * n + c + 1)
                else:
                    dve.wait_ge(used[S_O2 if n else S_OG], NR)
                s = slice(c * 2 * T, (c + 1) * 2 * T)
                tt(xt[:, s], A[c][:, :], xt[:, s], ALU.add).then_inc(x1_rdy, 1)

            for c in range(5):
                if c < 4:
                    residual(c, 0)
                if c > 0:
                    for k in (2 * c - 2, 2 * c - 1):
                        s = slice(k * T, (k + 1) * T)
                        dve.wait_ge(x1_rdy, KT + c)
                        dve.wait_ge(h_hi, KT + k + 1)
                        stt(hlo[:, s], xt[:, s], g_at[:, k:k + 1], f(hhi)[:, s], ALU.mult, ALU.subtract)\
                            .then_inc(h_lo, 1)
            dve.wait_ge(ss_done, 2)
            dve.wait_ge(i_in, 32)
            for t in range(TT):
                if t:
                    dve.wait_ge(rope_m, 2)
                stt(junk[:, :], W[1][:, t * P:(t + 1) * P], 1.0, ident, ALU.mult, ALU.mult,
                    accum_out=rtok[:, t:t + 1]).then_inc(rope_m, 1)
            dve.wait_ge(rope_m, 3)
            dve.sem_inc(rtok_rdy, 1)
            dve.wait_ge(std_rdy, 2)
            nc.vector.reciprocal(rtok[:, 2 * TT:3 * TT], rtok[:, TT:2 * TT]).then_inc(rtok_rdy, 1)
            dve.wait_ge(std_rdy, 3)
            nc.vector.reciprocal(rinv[:, :], std[:, :]).then_inc(rinv_rdy, 1)
            dve.wait_ge(rinv_rdy, 2)

            def silu_out(r):
                dve.wait_ge(o_done, r + 1)
                stt(yy[:, :], W[1][:, :], 0.5, sg[:, :], ALU.mult, ALU.mult).then_inc(y_rdy, 1)
                dve.wait_ge(yhi_rdy, NR + r + 1)
                tt(ylo[:, :], yy[:, :], f(yhi)[:, :], ALU.subtract).then_inc(ylo_rdy, 1)

            qk4 = qk[:, :].rearrange("p (t g d) -> p t g d", t=TT, g=4)
            x1v, x2v = qk4[:, :, :, 0:HALF], qk4[:, :, :, HALF:ROT]
            rt5 = rt[:, :].rearrange("p (i t g d) -> p i t g d", i=4, t=TT, g=4)

            def table(t):
                return t.rearrange("p (t a d) -> p t a d", t=TT, a=1).to_broadcast([P, TT, 4, HALF])

            def round2(r, first=False, last=False):
                n = r + NR
                split_lo(S_RV, n)
                if not first:
                    silu_out(r - 1)
                split_lo(S_OG, n)
                dve.wait_ge(q_rdy, r + 1)
                dve.wait_ge(k_rdy, r + 1)
                for i, (a, b) in enumerate(((x1v, cos_t), (x2v, sin_t), (x2v, cos_t), (x1v, sin_t))):
                    tt(rt5[:, i, :, :, :], a, table(b), ALU.mult).then_inc(rope_m, 1)
                dve.wait_ge(rope_m, 3 + 4 * r + 4)
                tt(x1v, rt5[:, 0, :, :, :], rt5[:, 1, :, :, :], ALU.subtract)
                tt(x2v, rt5[:, 2, :, :, :], rt5[:, 3, :, :, :], ALU.add).then_inc(rope_rdy, 1)
                if not first:
                    split_lo(S_O2, r - 1)
                dve.wait_ge(t_done, r + 1)
                nc.vector.tensor_copy(kT[:, :], W[1][:, :]).then_inc(kT_rdy, 1)
                if not last:
                    split_lo(S_XQ, n + 1)
                dve.wait_ge(used[S_OG], n + 1)
                tt(v3(gs, HT, T), v3(W[2], HT, T),
                   rinv[:, :].rearrange("p (a t) -> p a t", a=1).to_broadcast([P, HT, T]), ALU.mult)\
                    .then_inc(gs_rdy, 1)
                for h, b in ((0, 3), (1, 0)):
                    dve.wait_ge(s_done, 2 * r + h + 1)
                    dia = W[b][:, :].rearrange("p (n m) -> p n m", n=2)[:, :, 0:P]
                    tt(dia, dia, mask.rearrange("p (a m) -> p a m", a=1).to_broadcast([P, 2, P]), ALU.add)\
                        .then_inc(masked, 1)
                    dve.wait_ge(masked, 2 * r + h + 1)
                    nc.vector.reduce_max(mx[:, h * TT:h * TT + 1], W[b][:, 0:P], AX).then_inc(mx_rdy, 1)
                    nc.vector.reduce_max(mx[:, h * TT + 1:h * TT + 2], W[b][:, P:3 * P], AX).then_inc(mx_rdy, 1)
                    dve.wait_ge(mx_rdy, 4 * r + 2 * h + 2)
                    ts(nb[:, h * TT:(h + 1) * TT], mx[:, h * TT:(h + 1) * TT], -SCALE, None, ALU.mult)\
                        .then_inc(nb_rdy, 1)
                dve.wait_ge(tg_rdy, NR + r + 1)
                dve.wait_ge(gs_rdy, r + 1)
                stt(sg[:, :], tg[:, :], 1.0, gs[:, :], ALU.add, ALU.mult).then_inc(sg_rdy, 1)
                for h in range(HT):
                    dve.wait_ge(exp_rdy, 4 * r + 2 * h + 2)
                    nc.vector.reciprocal(rc[:, h * TT:(h + 1) * TT], rs[:, h * TT:(h + 1) * TT]).then_inc(rc_rdy, 1)
                    dve.wait_ge(rc_rdy, 2 * r + h + 1)
                    for t in range(TT):
                        s = slice(h * 3 * P, h * 3 * P + P) if t == 0 else slice(h * 3 * P + P, (h + 1) * 3 * P)
                        ts(pr[:, s], pr[:, s], rc[:, h * TT + t:h * TT + t + 1], None, ALU.mult).then_inc(pr_rdy, 1)
                if not last:
                    split_lo(S_GK, n + 1)
                dve.wait_ge(pT_done, 2 * r + 2)
                nc.vector.tensor_copy(pT[:, 3 * P:6 * P], W[2][:, 0:3 * P]).then_inc(pT_v, 1)

            round2(0, first=True)
            with dve.Fori(1, NR - 1) as r:
                round2(r)
            round2(NR - 1, last=True)
            split_lo(S_O2, NR - 1)
            silu_out(NR - 1)
            for c in range(4):
                residual(c, 1)
            dve.wait_ge(std_rdy, 4)
            nc.vector.reciprocal(rinv[:, :], std[:, :]).then_inc(rinv_rdy, 1)
            dve.wait_ge(rinv_rdy, 3)
            for k in range(KT):
                s = slice(k * T, (k + 1) * T)
                ins = stt(sq[:, s], xt[:, s], g_fin[:, k:k + 1], rinv[:, :], ALU.mult, ALU.mult)
                if k % 2:
                    ins.then_inc(out_rdy, 1)


def kernel(x, rg_norm, rg_w_in, rg_conv_w, rg_conv_b, rg_w_rgate, rg_b_rgate, rg_w_igate, rg_b_igate, rg_lambda,
           rg_w_out, at_norm, at_w_in, at_w_out, final_norm):
    import concourse.bacc as bacc
    from concourse.bass_utils import run_bass_kernel_spmd

    c = np.ascontiguousarray
    f32 = np.float32

    def chunks(w):
        n = w.shape[1] // CW
        return w.reshape(KT, P, n, CW).transpose(2, 1, 0, 3).reshape(n, P, CHUNK)

    def rows(w):
        return w.reshape(NR, HT, P, D).transpose(0, 2, 1, 3).reshape(NR, P, CHUNK)

    w_in, w_at = chunks(np.asarray(rg_w_in)[0]), chunks(np.asarray(at_w_in)[0])
    ri = np.stack([np.asarray(rg_w_rgate)[0], np.asarray(rg_w_igate)[0]], 2)
    ri = ri.reshape(NR, HT, P, 2 * CW).transpose(0, 2, 1, 3).reshape(NR, P, GCHUNK)
    per_channel = np.stack([*np.asarray(rg_conv_w)[0], np.asarray(rg_conv_b)[0], np.asarray(rg_b_rgate)[0].reshape(D),
                            np.asarray(rg_b_igate)[0].reshape(D), np.asarray(rg_lambda)[0]])
    inv_freq = f32(500000.0) ** (-np.arange(0, ROT, 2, dtype=f32) / f32(ROT))
    ang = np.arange(T, dtype=f32)[:, None] * inv_freq[None, :]
    rope = np.stack([np.cos(ang), np.sin(ang)]).astype(f32).reshape(2, TT, P, HALF).transpose(2, 0, 1, 3)
    causal = np.where(np.tril(np.ones((P, P), bool)), f32(0), f32(-3e38)).astype(f32)
    arrays = {
        "x_t": np.asarray(x)[0].T.reshape(KT, P, T).transpose(1, 0, 2).reshape(P, KT * T),
        "w_xq": np.concatenate([w_in[:NR], w_at[:NR]]),
        "w_gk": np.concatenate([w_in[NR:], w_at[NR:2 * NR]]),
        "w_ri": ri,
        "w_v": w_at[2 * NR:3 * NR],
        "w_og": np.concatenate([rows(np.asarray(rg_w_out)[0]), w_at[3 * NR:]]),
        "w_o2": rows(np.asarray(at_w_out)[0]),
        "consts": per_channel.reshape(NCONST, KT, P).transpose(2, 1, 0).reshape(P, KT * NCONST),
        "gains": np.stack([np.asarray(rg_norm)[0], np.asarray(at_norm)[0], np.asarray(final_norm)])
                   .reshape(3, KT, P).transpose(2, 0, 1).reshape(P, 3 * KT),
        "rope": rope.reshape(P, 2 * TT * HALF),
        "ident_mask": np.concatenate([np.eye(P, dtype=f32), causal], 1),
    }
    arrays = {k: c(v) for k, v in arrays.items()}
    nc = bacc.Bacc("TRN2", target_bir_lowering=False, num_devices=1)
    ins = [nc.dram_tensor(k, v.shape, mybir.dt.from_np(v.dtype), kind="ExternalInput").ap() for k, v in arrays.items()]
    out = nc.dram_tensor("out_t", (P, KT * T), F32, kind="ExternalOutput").ap()
    build(nc, *ins, out)
    r = run_bass_kernel_spmd(nc, [arrays], core_ids=[0])
    o = r.results[0]["out_t"]
    return o.reshape(P, KT, T).transpose(2, 1, 0).reshape(1, T, D)
```

```python
from contextlib import ExitStack

import numpy as np

import concourse.bass as bass
from concourse import mybir
from concourse.alu_op_type import AluOpType as ALU

D = 1024
T = 256
P = 128
KT = D // P
WARM = 14
NPIECE = 4
TT = T // P
NR = 4
CW = D // NR
HT = CW // P
TAPS = 4
ROT = 32
HALF = ROT // 2
EPS = 1e-6
SCALE = float(P) ** -0.5
NTERM = 8
NCONST = TAPS + 4
CHUNK = KT * CW
GCHUNK = HT * 2 * CW

S_XQ, S_GK, S_RV, S_OG, S_O2 = range(5)
NSLOT = 5

F32, F32R, BF16 = mybir.dt.float32, mybir.dt.float32r, mybir.dt.bfloat16
ACT = mybir.ActivationFunctionType
AX = mybir.AxisListType.X


def build(nc, x_t, w_xq, w_gk, w_ri, w_v, w_og, w_o2, consts, gains, rope, ident_mask, out_t):
    ctx = ExitStack()
    with ctx:
        def sb(name, cols, dt=F32):
            return ctx.enter_context(nc.sbuf_tensor(name, [P, cols], dt))

        def sem(name):
            return ctx.enter_context(nc.semaphore(name))

        raw = [sb(f"raw{j}", CHUNK) for j in range(NSLOT)]
        whi = [sb(f"whi{j}", CHUNK, F32R) for j in range(NSLOT)]
        wlo = [sb(f"wlo{j}", CHUNK, F32R) for j in range(NSLOT)]
        xt = sb("xt", KT * T)
        hhi, hlo = sb("hhi", KT * T, F32R), sb("hlo", KT * T, F32R)
        sq = sb("sq", KT * T)
        con = sb("con", NR * HT * NCONST)
        gn = sb("gn", 3 * KT)
        rp = sb("rp", 2 * TT * HALF)
        idm = sb("idm", 2 * P)
        ones = sb("ones", P)
        ssum = sb("ssum", T)
        xn, gs = sb("xn", HT * T), sb("gs", HT * T)
        zeros = sb("zeros", 2 * T, BF16)
        warm = sb("warm", 1)
        eps, minus1 = sb("eps", 1), sb("minus1", NR * HT)
        half_b = sb("half_b", NR * HT * 2)
        lam = sb("lam", 6 * NR * HT)
        c4 = sb("c4", NR * HT * 2)
        rinv = sb("rinv", T)
        rtok = sb("rtok", 2 * TT)
        diag = sb("diag", T)
        con_v, con_a = sb("con_v", HT * NCONST), sb("con_a", HT * NCONST)
        cb_a = sb("cb_a", HT * 4)
        xc = sb("xc", CW * HT)
        xchi, xclo = sb("xchi", HT * T, F32R), sb("xclo", HT * T, F32R)
        tr, ti, tg = sb("tr", HT * T), sb("ti", HT * T), sb("tg", HT * T)
        av, a2 = sb("av", HT * T), sb("a2", HT * T)
        mv, ix = sb("mv", HT * T), sb("ix", HT * T)
        uu, hh = sb("uu", HT * T), sb("hh", HT * T)
        sg, yy = sb("sg", HT * T), sb("yy", HT * T)
        yhi, ylo = sb("yhi", HT * T, F32R), sb("ylo", HT * T, F32R)
        qk = sb("qk", TT * 4 * P)
        rt, vv = mv, ix
        qT, kT = tr, ti
        pr = sb("pr", HT * 3 * P)
        pT = sb("pT", HT * 3 * P)
        mx, nb, rs, rc = (sb(n, HT * TT) for n in ("mx", "nb", "rs", "rc"))

        def psum(name):
            return ctx.enter_context(nc.psum_tensor(name, [P, 2 * T], F32))

        W = [psum(f"work{i}") for i in range(4)]
        A = [psum(f"acc{i}") for i in range(4)]

        def v3(t, n, m, at=0):
            return t[:, at:at + n * m].rearrange("p (n m) -> p n m", n=n)

        def f(t):
            return t.bitcast(F32)

        g_rg, g_at, g_fin = (gn[:, i * KT:(i + 1) * KT] for i in range(3))
        cos_t, sin_t = (rp[:, i * TT * HALF:(i + 1) * TT * HALF] for i in range(2))
        ident, mask = idm[:, 0:P], idm[:, P:2 * P]

        raw_in = [sem(f"raw_in{j}") for j in range(NSLOT)]
        x_in = [sem(f"x_in{c}") for c in range(NPIECE)]
        w0_in = [sem(f"w0_in{c}") for c in range(2)]
        hi_rdy = [sem(f"hi_rdy{j}") for j in range(NSLOT)]
        lo_rdy = [sem(f"lo_rdy{j}") for j in range(NSLOT)]
        used = [sem(f"used{j}") for j in range(NSLOT)]
        (c_in, i_in, half_hi, half_lo, diag_rdy, rb_done, rb_rdy, const_rdy, sq_rdy, ss_done, std_rdy, h_hi, h_lo, c4_rdy, ssum_step, gn_rdy, xn_rdy, lam_abs, lam_step, hb_rdy, e_lam,
         zero_done, con_v_rdy, con_a_rdy, cb_a_rdy, r_done, out_done, xc_init, conv_step, xchi_rdy,
         xclo_rdy, tr_rdy, ti_rdy, tg_rdy, a_rdy, a2_rdy, a2c_rdy, m_rdy, ix_rdy, u_rdy, scan_rdy, sg_rdy, y_rdy,
         yhi_rdy, ylo_rdy, x1_rdy, rtok_rdy, q_rdy, k_rdy, v_rdy, rope_m, rope_rdy, t_done,
         qT_rdy, kT_rdy, s_done, masked, mx_rdy, nb_rdy, exp_rdy, rc_rdy, pr_rdy, pT_done, pT_a,
         pT_v, o_done, out_w, out_rdy) = (sem(n) for n in (
             "c_in i_in half_hi half_lo diag_rdy rb_done rb_rdy const_rdy sq_rdy ss_done std_rdy h_hi h_lo c4_rdy ssum_step gn_rdy xn_rdy lam_abs lam_step hb_rdy e_lam "
             "zero_done con_v_rdy con_a_rdy cb_a_rdy r_done out_done xc_init conv_step xchi_rdy "
             "xclo_rdy tr_rdy ti_rdy tg_rdy a_rdy a2_rdy a2c_rdy m_rdy ix_rdy u_rdy scan_rdy sg_rdy y_rdy "
             "yhi_rdy ylo_rdy x1_rdy rtok_rdy q_rdy k_rdy v_rdy rope_m rope_rdy t_done "
             "qT_rdy kT_rdy s_done masked mx_rdy nb_rdy exp_rdy rc_rdy pr_rdy pT_done pT_a "
             "pT_v o_done out_w out_rdy").split())

        block = ctx.enter_context(nc.Block())

        @block.sync
        def _(sp):
            def load(j, n, dram, at, words=CHUNK, first=False):
                if not first:
                    sp.wait_ge(hi_rdy[j], n)
                    sp.wait_ge(lo_rdy[j], n)
                sp.dma_start(raw[j][:, 0:words],
                             dram[bass.ds(at, 1), :, :].rearrange("a p c -> p (a c)")).then_inc(raw_in[j], 16)

            for c in range(NPIECE):
                w = slice(c * KT * T // NPIECE, (c + 1) * KT * T // NPIECE)
                sp.dma_start(xt[:, w], x_t[:, w]).then_inc(x_in[c], 16)
                if c % 2:
                    w = slice(c // 2 * CHUNK // 2, (c // 2 + 1) * CHUNK // 2)
                    sp.dma_start(raw[S_XQ][:, w], w_xq[0, :, w]).then_inc(w0_in[c // 2], 16)
            load(S_GK, 0, w_gk, 0, first=True)
            load(S_RV, 0, w_ri, 0, GCHUNK, first=True)
            load(S_XQ, 1, w_xq, 1)
            load(S_GK, 1, w_gk, 1)
            load(S_RV, 1, w_ri, 1, GCHUNK)
            load(S_XQ, 2, w_xq, 2)
            load(S_OG, 0, w_og, 0, first=True)
            load(S_O2, 0, w_o2, 0, first=True)
            for r in range(1, NR):
                if r == 1:
                    load(S_GK, r + 1, w_gk, r + 1)
                else:
                    load(S_OG, r - 1, w_og, r - 1)
                load(S_XQ, r + 2, w_xq, r + 2)
                if r > 1:
                    load(S_GK, r + 1, w_gk, r + 1)
                load(S_RV, r + 1, *((w_ri, r + 1, GCHUNK) if r < NR - 1 else (w_v, 0)))
            load(S_OG, NR - 1, w_og, NR - 1)
            load(S_O2, 1, w_o2, 1)
            load(S_GK, 5, w_gk, 5)
            load(S_RV, NR + 1, w_v, 1)
            load(S_OG, 4, w_og, 4)
            for r in range(2, NR):
                load(S_XQ, NR + r, w_xq, NR + r)
                if r == 2:
                    load(S_GK, NR + r, w_gk, NR + r)
                    load(S_RV, NR + r, w_v, r)
                    load(S_OG, NR + r - 1, w_og, NR + r - 1)
                    load(S_O2, r, w_o2, r)
            load(S_GK, 7, w_gk, 7)
            load(S_RV, NR + 3, w_v, 3)
            load(S_OG, 6, w_og, 6)
            load(S_O2, 3, w_o2, 3)
            load(S_XQ, 8, w_xq, 8)
            for c in range(4):
                sp.wait_ge(out_rdy, c + 1)
                sp.dma_start(out_t[:, c * 2 * T:(c + 1) * 2 * T], sq[:, c * 2 * T:(c + 1) * 2 * T]).then_inc(out_w, 16)
            sp.wait_ge(out_w, 4 * 16)

        @block.gpsimd
        def _(pool):
            pool.memset(zeros[:, :], 0.0).then_inc(const_rdy, 1)
            pool.memset(ones[:, :], 1.0).then_inc(const_rdy, 1)
            pool.memset(eps[:, :], EPS).then_inc(const_rdy, 1)
            pool.memset(minus1[:, :], -1.0).then_inc(const_rdy, 1)
            ts, tt = pool.tensor_scalar, pool.tensor_tensor
            pool.wait_ge(c_in, 32)
            L8 = NR * HT
            con3 = v3(con, L8, NCONST)
            lam_in = con3[:, :, NCONST - 1]
            L = [lam[:, i * L8:(i + 1) * L8] for i in range(6)]
            steps = 0

            def chain(ins):
                nonlocal steps
                steps += 1
                ins.then_inc(lam_step, 1)
                pool.wait_ge(lam_step, steps)

            ts(v3(half_b, L8, 2), con3[:, :, TAPS + 1:TAPS + 3], 0.5, None, ALU.mult).then_inc(hb_rdy, 1)
            chain(ts(L[5], lam_in, 0.0, None, ALU.min))
            chain(ts(L[2], lam_in, 0.0, None, ALU.max))
            tt(L[0], L[5], L[2], ALU.subtract).then_inc(lam_abs, 1)

            def log_sigmoid():
                pool.wait_ge(e_lam, 1)
                e = L[1]
                chain(ts(L[2], e, 2.0, None, ALU.add))
                chain(tt(L[3], L[2], minus1[:, :], ALU.pow))
                chain(tt(L[2], e, L[3], ALU.mult))
                chain(tt(L[3], L[2], L[2], ALU.mult))
                chain(ts(L[4], L[3], 1.0 / (2 * NTERM + 1), 1.0 / (2 * NTERM - 1), ALU.mult, ALU.add))
                for i in range(NTERM - 2, -1, -1):
                    chain(tt(L[4], L[4], L[3], ALU.mult))
                    chain(ts(L[4], L[4], 1.0 / (2 * i + 1), None, ALU.add))
                chain(tt(L[4], L[4], L[2], ALU.mult))
                chain(ts(L[4], L[4], -2.0, None, ALU.mult))
                chain(tt(L[4], L[4], L[5], ALU.add))
                c43 = v3(c4, L8, 2)
                ts(c43[:, :, 0], L[4], 4.0, None, ALU.mult).then_inc(c4_rdy, 1)
                ts(c43[:, :, 1], L[4], 8.0, None, ALU.mult).then_inc(c4_rdy, 1)

            log_sigmoid()
            for n in range(2):
                for k in range(1, KT):
                    pool.wait_ge(sq_rdy, n * NPIECE + k // 2 + 1)
                    if k == 1 and n:
                        pool.wait_ge(ss_done, n)
                    if k > 1:
                        pool.wait_ge(ssum_step, n * (KT - 1) + k - 1)
                    a = sq[:, 0:T] if k == 1 else ssum[:, :]
                    pool.tensor_tensor(ssum[:, :], a, sq[:, k * T:(k + 1) * T], ALU.add).then_inc(ssum_step, 1)

        @block.tensor
        def _(pe):
            def mm(o, w, x, start=False, stop=False):
                return pe.matmul(o, w, x, start=start, stop=stop, skip_group_check=True)

            def split3(o, ahi, alo, bhi, blo, start, stop):
                mm(o, ahi, bhi, start=start)
                mm(o, ahi, blo)
                return mm(o, alo, bhi, stop=stop)

            def chunk_ready(j, n):
                pe.wait_ge(hi_rdy[j], n + 1)
                pe.wait_ge(lo_rdy[j], n + 1)

            def project(j, n, bank, wait_h=0, between=None, at=KT // 2, halves=False):
                if not halves:
                    chunk_ready(j, n)
                for k in range(KT):
                    if between and k == at:
                        between()
                    if halves and k % (KT // 2) == 0:
                        pe.wait_ge(half_hi, 2 * n + 2 * k // KT + 1)
                        pe.wait_ge(half_lo, 2 * n + 2 * k // KT + 1)
                    if wait_h:
                        pe.wait_ge(h_hi, (wait_h - 1) * KT + k + 1)
                        pe.wait_ge(h_lo, (wait_h - 1) * KT + k + 1)
                    for m in range(HT):
                        w = slice(k * CW + m * P, k * CW + m * P + P)
                        h = slice(k * T, (k + 1) * T)
                        last = split3(bank[:, m * T:(m + 1) * T], whi[j][:, w], wlo[j][:, w], hhi[:, h], hlo[:, h],
                                      k == 0 and m == 0, k == KT - 1)
                last.then_inc(used[j], 1)

            def project_tok(j, n, bank, wait_h=0, between=None):
                chunk_ready(j, n)
                for k in range(KT):
                    if between and k == KT // 2:
                        between()
                    if wait_h:
                        pe.wait_ge(h_hi, (wait_h - 1) * KT + k + 1)
                        pe.wait_ge(h_lo, (wait_h - 1) * KT + k + 1)
                    for t in range(TT):
                        w = slice(k * CW, (k + 1) * CW)
                        h = slice(k * T + t * P, k * T + t * P + P)
                        last = split3(bank[:, t * CW:(t + 1) * CW], hhi[:, h], hlo[:, h], whi[j][:, w], wlo[j][:, w],
                                      k == 0 and t == 0, k == KT - 1)
                last.then_inc(used[j], 1)

            def clear_acc():
                for a in A:
                    last = mm(a[:, :], zeros[:, 0:P], zeros[:, :], start=True)
                last.then_inc(zero_done, 1)

            def project_out(j, n, yn, last_of_layer=False, y_hi=yhi, y_lo=ylo):
                chunk_ready(j, n)
                pe.wait_ge(yhi_rdy, yn + 1)
                pe.wait_ge(ylo_rdy, yn + 1)
                for c in range(KT):
                    for k in range(HT):
                        w = slice(k * D + c * P, k * D + c * P + P)
                        y = slice(k * T, (k + 1) * T)
                        last = split3(A[c // 2][:, (c % 2) * T:(c % 2 + 1) * T], whi[j][:, w], wlo[j][:, w],
                                      y_hi[:, y], y_lo[:, y], False, last_of_layer and k == HT - 1)
                    if last_of_layer and c % 2 == 1 and c < KT - 1:
                        last.then_inc(out_done, 1)
                last.then_inc(used[j], 1)

            def sum_squares(n, bank):
                pe.wait_ge(ssum_step, (n + 1) * (KT - 1))
                for t in range(TT):
                    last = mm(bank[:, t:t + 1], ssum[:, t * P:(t + 1) * P], ones[:, 0:1], start=t == 0, stop=True)
                last.then_inc(ss_done, 1)

            def sum_all_squares():
                for k in range(KT):
                    if k % 2 == 0:
                        pe.wait_ge(sq_rdy, 2 * NPIECE + k // 2 + 1)
                    for t in range(TT):
                        last = mm(W[1][:, t:t + 1], sq[:, k * T + t * P:k * T + (t + 1) * P], ones[:, 0:1],
                                  start=k == 0 and t == 0, stop=k == KT - 1)
                last.then_inc(ss_done, 1)

            def broadcast_rms(n, bank):
                pe.wait_ge(diag_rdy, n + 1)
                mm(bank[:, 0:T], ones[:, :], diag[:, :], start=True, stop=True).then_inc(rb_done, 1)

            pe.wait_ge(const_rdy, 1)
            for i in range(WARM):
                mm(W[3][:, :], zeros[:, 0:P], zeros[:, :], start=True, stop=True)

            def gates(r, first=False):
                chunk_ready(S_RV, r)
                pe.wait_ge(xchi_rdy, r + 1)
                pe.wait_ge(xclo_rdy, r + 1)
                if first:
                    pe.wait_ge(rb_rdy, 1)
                else:
                    pe.wait_ge(tr_rdy, r)
                    pe.wait_ge(ti_rdy, r)
                for g in range(2):
                    for m in range(HT):
                        for k in range(HT):
                            w = slice(k * 2 * CW + g * CW + m * P, k * 2 * CW + g * CW + m * P + P)
                            x = slice(k * T, (k + 1) * T)
                            last = split3(W[2 + g][:, m * T:(m + 1) * T], whi[S_RV][:, w], wlo[S_RV][:, w],
                                          xchi[:, x], xclo[:, x], m == 0 and k == 0, k == HT - 1)
                    last.then_inc(used[S_RV] if g else r_done, 1)

            def next_branch(r):
                pe.wait_ge(xn_rdy, r)
                project(S_XQ, r, W[0])

            def this_gate(r):
                pe.wait_ge(gn_rdy, r)
                project(S_GK, r, W[1])

            project(S_XQ, 0, W[0], wait_h=1, halves=True)
            project(S_GK, 0, W[1], between=lambda: sum_squares(0, W[3]), at=5)
            broadcast_rms(0, W[3])
            project(S_XQ, 1, A[3], halves=True)
            gates(0, first=True)
            pe.wait_ge(xn_rdy, 2)
            clear_acc()
            with pe.Fori(1, NR - 1) as r:
                next_branch(r + 1)
                this_gate(r)
                gates(r)
                project_out(S_OG, r - 1, r - 1)
            this_gate(NR - 1)
            gates(NR - 1)
            project_out(S_OG, NR - 2, NR - 2)
            project_out(S_O2, 0, NR - 1, last_of_layer=True, y_hi=xchi, y_lo=xclo)

            def pv(r):
                pe.wait_ge(pT_a, r + 1)
                pe.wait_ge(pT_v, r + 1)
                for h in range(HT):
                    mm(W[1][:, h * T:(h + 1) * T], vv[:, h * P:(h + 1) * P], pT[:, h * 3 * P:h * 3 * P + T], start=True)
                    last = mm(W[1][:, h * T + P:(h + 1) * T], vv[:, CW + h * P:CW + (h + 1) * P],
                              pT[:, h * 3 * P + T:(h + 1) * 3 * P], stop=True)
                last.then_inc(o_done, 1)

            def round2(r, first=False):
                n = r + NR
                if not first:
                    pe.wait_ge(exp_rdy, 4 * r)
                else:
                    pe.wait_ge(xn_rdy, NR)
                project_tok(S_XQ, n, W[0], wait_h=2 if first else 0)
                if first:
                    pe.wait_ge(gn_rdy, NR)
                    sum_squares(1, W[1])
                    pe.wait_ge(tr_rdy, NR)
                    pe.wait_ge(ti_rdy, NR)
                    project_tok(S_GK, n, W[2], between=lambda: broadcast_rms(1, W[1]))
                    clear_acc()
                else:
                    pv(r - 1)
                    pe.wait_ge(pT_v, r)
                    project_tok(S_GK, n, W[2])
                if not first:
                    pe.wait_ge(masked, 2 * r)
                    pe.wait_ge(exp_rdy, 4 * r)
                project_tok(S_RV, n, W[3])
                pe.wait_ge(rope_rdy, r + 1)
                if first:
                    pe.wait_ge(rb_rdy, 2)
                else:
                    pe.wait_ge(y_rdy, r + NR)
                for b, g0 in ((0, 0), (1, 2)):
                    for h in range(HT):
                        for t in range(TT):
                            last = pe.transpose(W[b][:, h * T + t * P:h * T + (t + 1) * P],
                                                qk[:, (t * 4 + g0 + h) * P:(t * 4 + g0 + h + 1) * P], ident)
                last.then_inc(t_done, 1)
                pe.wait_ge(k_rdy, r + 1)
                project(S_OG, n - 1, W[2])
                pe.wait_ge(qT_rdy, r + 1)
                pe.wait_ge(kT_rdy, r + 1)
                pe.wait_ge(v_rdy, r + 1)
                for h, b in ((0, 3), (1, 0)):
                    mm(W[b][:, 0:P], qT[:, h * T:h * T + P], kT[:, h * T:h * T + P], start=True, stop=True)
                    mm(W[b][:, P:3 * P], qT[:, h * T + P:(h + 1) * T], kT[:, h * T:(h + 1) * T],
                       start=True, stop=True).then_inc(s_done, 1)
                if not first:
                    project_out(S_O2, r, NR + r - 1)
                pe.wait_ge(gn_rdy, n + 1)
                for h in range(HT):
                    pe.wait_ge(pr_rdy, 4 * r + 2 * h + 2)
                    for i in range(3):
                        s = slice((h * 3 + i) * P, (h * 3 + i + 1) * P)
                        last = pe.transpose(W[1 + h][:, i * P:(i + 1) * P], pr[:, s], ident)
                    last.then_inc(pT_done, 1)

            round2(0, first=True)
            with pe.Fori(1, NR) as r:
                round2(r)
            pv(NR - 1)
            project_out(S_XQ, 2 * NR, 2 * NR - 1, last_of_layer=True)
            pe.wait_ge(y_rdy, 2 * NR)
            sum_all_squares()
            broadcast_rms(2, W[1])

        @block.scalar
        def _(act):
            def split_hi(j, n, words=CHUNK, slot_free=False):
                act.wait_ge(raw_in[j], 16 * n if j == S_XQ else 16 * n + 16)
                if not slot_free:
                    act.wait_ge(used[j], n)
                nc.scalar.activation(whi[j][:, 0:words], raw[j][:, 0:words], ACT.Copy).then_inc(hi_rdy[j], 1)

            act.dma_start(con[:, :], consts).then_inc(c_in, 16)
            act.dma_start(gn[:, :], gains).then_inc(c_in, 16)
            act.dma_start(idm[:, :], ident_mask).then_inc(i_in, 16)
            act.dma_start(rp[:, :], rope).then_inc(i_in, 16)
            act.wait_ge(const_rdy, 3)
            nc.scalar.activation(warm[:, :], eps[:, :], ACT.Exp)
            act.wait_ge(lam_abs, 1)
            L8 = NR * HT
            nc.scalar.activation(lam[:, L8:2 * L8], lam[:, 0:L8], ACT.Exp).then_inc(e_lam, 1)

            act.wait_ge(c_in, 32)

            def h_high(k, gain):
                nc.scalar.activation(hhi[:, k * T:(k + 1) * T], xt[:, k * T:(k + 1) * T], ACT.Copy,
                                     scale=gain[:, k:k + 1]).then_inc(h_hi, 1)

            def squares(c):
                s = slice(c * KT * T // NPIECE, (c + 1) * KT * T // NPIECE)
                nc.scalar.activation(sq[:, s], xt[:, s], ACT.Square).then_inc(sq_rdy, 1)

            for c in range(NPIECE):
                act.wait_ge(x_in[c], 16)
                h_high(2 * c, g_rg)
                h_high(2 * c + 1, g_rg)
                if c % 2:
                    w = slice(c // 2 * CHUNK // 2, (c // 2 + 1) * CHUNK // 2)
                    act.wait_ge(w0_in[c // 2], 16)
                    nc.scalar.activation(whi[S_XQ][:, w], raw[S_XQ][:, w], ACT.Copy).then_inc(half_hi, 1)
            act.wait_ge(half_hi, 2)
            act.sem_inc(hi_rdy[S_XQ], 1)
            squares(0)
            split_hi(S_GK, 0, slot_free=True)
            for c in range(1, NPIECE):
                squares(c)
            split_hi(S_RV, 0, GCHUNK, slot_free=True)
            for c in range(2):
                w = slice(c * CHUNK // 2, (c + 1) * CHUNK // 2)
                act.wait_ge(raw_in[S_XQ], 16)
                act.wait_ge(used[S_XQ], 1)
                nc.scalar.activation(whi[S_XQ][:, w], raw[S_XQ][:, w], ACT.Copy).then_inc(half_hi, 1)
            act.wait_ge(half_hi, 4)
            act.sem_inc(hi_rdy[S_XQ], 1)
            nc.scalar.activation(warm[:, :], eps[:, :], ACT.Sqrt)

            def rms(n, bank):
                act.wait_ge(ss_done, n + 1)
                nc.scalar.activation(rtok[:, 0:TT], bank[:, 0:TT], ACT.Sqrt, bias=eps[:, :], scale=1.0 / D)\
                    .then_inc(std_rdy, 1)

            def keep_rms(n, bank):
                act.wait_ge(rb_done, n + 1)
                nc.scalar.activation(rinv[:, :], bank[:, 0:T], ACT.Copy).then_inc(rb_rdy, 1)

            rms(0, W[3])
            keep_rms(0, W[3])
            act.wait_ge(hb_rdy, 1)

            def conv_constants(r):
                nc.scalar.activation(con_a[:, :], v3(con, NR, HT * NCONST)[:, bass.ds(r, 1), :]
                                     .rearrange("p a c -> p (a c)"), ACT.Copy).then_inc(con_a_rdy, 1)
                act.wait_ge(con_a_rdy, r + 1)

            def gate_constants(r):
                for src, at in ((half_b, 0), (c4, HT * 2)):
                    nc.scalar.activation(cb_a[:, at:at + HT * 2], v3(src, NR, HT * 2)[:, bass.ds(r, 1), :]
                                         .rearrange("p a c -> p (a c)"), ACT.Copy).then_inc(cb_a_rdy, 1)
                act.wait_ge(cb_a_rdy, 2 * r + 2)

            def conv_start(r):
                act.wait_ge(xn_rdy, r + 1)
                for m in range(HT):
                    c0 = m * NCONST
                    nc.scalar.activation(xc[:, m * T:(m + 1) * T], xn[:, m * T:(m + 1) * T], ACT.Identity,
                                         bias=con_a[:, c0 + TAPS:c0 + TAPS + 1],
                                         scale=con_a[:, c0 + TAPS - 1:c0 + TAPS]).then_inc(xc_init, 1)

            def conv_high(r):
                act.wait_ge(conv_step, 6 * r + 6)
                nc.scalar.activation(xchi[:, :], xc[:, :], ACT.Copy).then_inc(xchi_rdy, 1)

            conv_constants(0)
            conv_start(0)
            split_hi(S_GK, 1)
            conv_high(0)
            act.wait_ge(c4_rdy, 2)
            nc.scalar.activation(warm[:, :], eps[:, :], ACT.Exp)

            def round1(r, first=False, last=False):
                def gate_tanh():
                    act.wait_ge(gn_rdy, r + 1)
                    if not first:
                        act.wait_ge(sg_rdy, r)
                    nc.scalar.activation(tg[:, :], gs[:, :], ACT.Tanh, scale=0.5).then_inc(tg_rdy, 1)

                if not first:
                    act.wait_ge(a_rdy, HT * r)
                gate_constants(r)
                if last:
                    split_hi(S_O2, 0, slot_free=True)
                    gate_tanh()
                else:
                    split_hi(S_XQ, r + 2)
                for g, (t, rdy) in enumerate(((tr, tr_rdy), (ti, ti_rdy))):
                    act.wait_ge(used[S_RV] if g else r_done, r + 1)
                    if g == 1 and not first:
                        act.wait_ge(ix_rdy, r)
                    for m in range(HT):
                        ins = nc.scalar.activation(t[:, m * T:(m + 1) * T], W[2 + g][:, m * T:(m + 1) * T], ACT.Tanh,
                                                   bias=cb_a[:, m * 2 + g:m * 2 + g + 1], scale=0.5)
                    ins.then_inc(rdy, 1)
                act.wait_ge(tr_rdy, r + 1)
                if not first:
                    act.wait_ge(scan_rdy, HT * r)
                    act.wait_ge(m_rdy, r)
                for i, (dst, rdy) in enumerate(((a2, a2_rdy), (av, a_rdy))):
                    for m in range(HT):
                        c = cb_a[:, HT * 2 + m * 2 + 1 - i:HT * 2 + m * 2 + 2 - i]
                        nc.scalar.activation(dst[:, m * T:(m + 1) * T], tr[:, m * T:(m + 1) * T], ACT.Exp,
                                             bias=c, scale=c).then_inc(rdy, 1)
                if not last:
                    gate_tanh()
                    act.wait_ge(conv_step, 6 * r + 6)
                    conv_constants(r + 1)
                    act.wait_ge(ix_rdy, r + 1)
                    conv_start(r + 1)
                    if not first:
                        split_hi(S_GK, r + 1)
                act.wait_ge(a2c_rdy, r + 1)
                if not first:
                    act.wait_ge(u_rdy, r)
                nc.scalar.activation(mv[:, :], a2[:, :], ACT.Sqrt, bias=1.0, scale=-1.0).then_inc(m_rdy, 1)
                if not last:
                    act.wait_ge(used[S_RV], r + 1)
                    conv_high(r + 1)
                    split_hi(S_RV, r + 1, GCHUNK, slot_free=True)
                    split_hi(S_OG, r, slot_free=first)
                act.wait_ge(y_rdy, r + 1)
                nc.scalar.activation((xchi if last else yhi)[:, :], yy[:, :], ACT.Copy).then_inc(yhi_rdy, 1)
                if last:
                    split_hi(S_GK, r + 1)

            round1(0, first=True)
            with act.Fori(1, NR - 1) as r:
                round1(r)
            round1(NR - 1, last=True)

            act.wait_ge(used[S_GK], NR)
            for c in range(NPIECE):
                act.wait_ge(x1_rdy, c + 1)
                h_high(2 * c, g_at)
                h_high(2 * c + 1, g_at)
                squares(c)
            rms(1, W[1])
            split_hi(S_RV, NR)
            act.wait_ge(rtok_rdy, 2)

            def token_scaled(dst, bank, rdy):
                for t in range(TT):
                    ins = nc.scalar.activation(dst(t), bank[:, t * CW:(t + 1) * CW], ACT.Copy,
                                               scale=rtok[:, TT + t:TT + t + 1])
                ins.then_inc(rdy, 1)

            def round2(r, first=False, last=False):
                n = r + NR
                act.wait_ge(used[S_XQ], n + 1)
                if not first:
                    act.wait_ge(t_done, r)
                token_scaled(lambda t: qk[:, t * 4 * P:t * 4 * P + CW], W[0], q_rdy)
                if first:
                    split_hi(S_OG, n - 1)
                    keep_rms(1, W[1])
                else:
                    split_hi(S_RV, n)
                    act.wait_ge(y_rdy, n)
                    nc.scalar.activation(yhi[:, :], yy[:, :], ACT.Copy).then_inc(yhi_rdy, 1)
                    split_hi(S_OG, n - 1)
                act.wait_ge(used[S_GK], n + 1)
                token_scaled(lambda t: qk[:, t * 4 * P + CW:(t + 1) * 4 * P], W[2], k_rdy)
                if not first:
                    split_hi(S_O2, r, slot_free=True)
                act.wait_ge(used[S_RV], n + 1)
                if not first:
                    act.wait_ge(o_done, r)
                token_scaled(lambda t: vv[:, t * CW:(t + 1) * CW], W[3], v_rdy)
                act.wait_ge(t_done, r + 1)
                if not first:
                    act.wait_ge(s_done, 2 * r)
                nc.scalar.activation(qT[:, :], W[0][:, :], ACT.Copy).then_inc(qT_rdy, 1)
                split_hi(S_XQ, n + 1)
                act.wait_ge(gn_rdy, n + 1)
                nc.scalar.activation(tg[:, :], gs[:, :], ACT.Tanh, scale=0.5).then_inc(tg_rdy, 1)
                for h, b in ((0, 3), (1, 0)):
                    act.wait_ge(nb_rdy, 2 * r + h + 1)
                    if not first:
                        act.wait_ge(pT_done, 2 * r)
                        act.wait_ge(rc_rdy, 2 * r)
                    for t in range(TT):
                        s = slice(0, P) if t == 0 else slice(P, 3 * P)
                        nc.scalar.activation(pr[:, h * 3 * P + s.start:h * 3 * P + s.stop], W[b][:, s], ACT.Exp,
                                             bias=nb[:, h * TT + t:h * TT + t + 1], scale=SCALE,
                                             accum_out=rs[:, h * TT + t:h * TT + t + 1]).then_inc(exp_rdy, 1)
                if not last:
                    split_hi(S_GK, n + 1)
                act.wait_ge(pT_done, 2 * r + 1)
                if not first:
                    act.wait_ge(o_done, r)
                nc.scalar.activation(pT[:, 0:3 * P], W[1][:, 0:3 * P], ACT.Copy).then_inc(pT_a, 1)

            round2(0, first=True)
            with act.Fori(1, NR - 1) as r:
                round2(r)
            round2(NR - 1, last=True)
            act.wait_ge(y_rdy, 2 * NR)
            nc.scalar.activation(yhi[:, :], yy[:, :], ACT.Copy).then_inc(yhi_rdy, 1)

            for c in range(NPIECE):
                act.wait_ge(x1_rdy, NPIECE + c + 1)
                squares(c)
            rms(2, W[1])

        @block.vector
        def _(dve):
            tt, stt, ts = nc.vector.tensor_tensor, nc.vector.scalar_tensor_tensor, nc.vector.tensor_scalar

            def split_lo(j, n, words=CHUNK):
                dve.wait_ge(hi_rdy[j], n + 1)
                tt(wlo[j][:, 0:words], raw[j][:, 0:words], f(whi[j])[:, 0:words], ALU.subtract)\
                    .then_inc(lo_rdy[j], 1)

            dve.wait_ge(c_in, 32)

            def h_low(k, gain, n):
                s = slice(k * T, (k + 1) * T)
                dve.wait_ge(h_hi, n * KT + k + 1)
                stt(hlo[:, s], xt[:, s], gain[:, k:k + 1], f(hhi)[:, s], ALU.mult, ALU.subtract).then_inc(h_lo, 1)

            for c in range(2):
                for k in range(c * KT // 2, (c + 1) * KT // 2):
                    h_low(k, g_rg, 0)
                w = slice(c * CHUNK // 2, (c + 1) * CHUNK // 2)
                dve.wait_ge(half_hi, c + 1)
                tt(wlo[S_XQ][:, w], raw[S_XQ][:, w], f(whi[S_XQ])[:, w], ALU.subtract).then_inc(half_lo, 1)
            dve.wait_ge(half_lo, 2)
            dve.sem_inc(lo_rdy[S_XQ], 1)
            split_lo(S_GK, 0)
            def inverse_rms(n):
                dve.wait_ge(std_rdy, n + 1)
                if n:
                    dve.wait_ge(rb_done, n)
                nc.vector.reciprocal(rtok[:, TT:2 * TT], rtok[:, 0:TT]).then_inc(rtok_rdy, 1)
                dve.wait_ge(rtok_rdy, n + 1)
                for t in range(TT):
                    ins = ts(diag[:, t * P:(t + 1) * P], ident, rtok[:, TT + t:TT + t + 1], None, ALU.mult)
                ins.then_inc(diag_rdy, 1)

            split_lo(S_RV, 0, GCHUNK)
            dve.wait_ge(i_in, 32)
            for c in range(2):
                w = slice(c * CHUNK // 2, (c + 1) * CHUNK // 2)
                dve.wait_ge(half_hi, 3 + c)
                tt(wlo[S_XQ][:, w], raw[S_XQ][:, w], f(whi[S_XQ])[:, w], ALU.subtract).then_inc(half_lo, 1)
                if c == 0:
                    inverse_rms(0)
            dve.wait_ge(half_lo, 4)
            dve.sem_inc(lo_rdy[S_XQ], 1)

            def normalise(dst, bank):
                return tt(v3(dst, HT, T), v3(bank, HT, T),
                          rinv[:, :].rearrange("p (a t) -> p a t", a=1).to_broadcast([P, HT, T]), ALU.mult)

            def branch(r, bank):
                dve.wait_ge(used[S_XQ], r + 1)
                normalise(xn, bank).then_inc(xn_rdy, 1)

            def gate(r):
                dve.wait_ge(used[S_GK], r + 1)
                normalise(gs, W[1]).then_inc(gn_rdy, 1)

            def conv(r):
                nc.vector.tensor_copy(con_v[:, :], v3(con, NR, HT * NCONST)[:, bass.ds(r, 1), :]
                                      .rearrange("p a c -> p (a c)")).then_inc(con_v_rdy, 1)
                dve.wait_ge(con_v_rdy, r + 1)
                dve.wait_ge(xn_rdy, r + 1)
                for i in range(1, TAPS):
                    for m in range(HT):
                        dve.wait_ge(xc_init, HT * r + m + 1)
                        if i > 1:
                            dve.wait_ge(conv_step, 6 * r + (i - 2) * HT + m + 1)
                        c = m * NCONST + TAPS - 1 - i
                        o = xc[:, m * T + i:(m + 1) * T]
                        stt(o, xn[:, m * T:(m + 1) * T - i], con_v[:, c:c + 1], o, ALU.mult, ALU.add)\
                            .then_inc(conv_step, 1)

            def conv_low(r):
                dve.wait_ge(xchi_rdy, r + 1)
                tt(xclo[:, :], xc[:, :], f(xchi)[:, :], ALU.subtract).then_inc(xclo_rdy, 1)

            dve.wait_ge(rb_rdy, 1)
            branch(0, W[0])
            gate(0)
            conv(0)
            conv_low(0)
            split_lo(S_GK, 1)

            def round1(r, first=False, last=False):
                if not first:
                    split_lo(S_OG, r - 1)

                def gate_silu():
                    dve.wait_ge(tg_rdy, r + 1)
                    dve.wait_ge(gn_rdy, r + 1)
                    stt(sg[:, :], tg[:, :], 1.0, gs[:, :], ALU.add, ALU.mult).then_inc(sg_rdy, 1)

                if not last:
                    branch(r + 1, A[3] if first else W[0])
                    split_lo(S_XQ, r + 2)
                if not first:
                    gate(r)
                dve.wait_ge(ti_rdy, r + 1)
                if not first:
                    dve.wait_ge(u_rdy, r)
                stt(ix[:, :], ti[:, :], 1.0, xc[:, :], ALU.add, ALU.mult).then_inc(ix_rdy, 1)
                dve.wait_ge(a2_rdy, HT * (r + 1))
                ts(a2[:, :], a2[:, :], 1.0, None, ALU.min).then_inc(a2c_rdy, 1)
                gate_silu()
                if last:
                    split_lo(S_O2, 0)
                else:
                    conv(r + 1)
                    if not first:
                        split_lo(S_GK, r + 1)
                    conv_low(r + 1)
                dve.wait_ge(m_rdy, r + 1)
                dve.wait_ge(ix_rdy, r + 1)
                stt(uu[:, :], mv[:, :], 0.5, ix[:, :], ALU.mult, ALU.mult).then_inc(u_rdy, 1)
                dve.wait_ge(u_rdy, r + 1)
                dve.wait_ge(a_rdy, HT * (r + 1))
                for m in range(HT):
                    s = slice(m * T, (m + 1) * T)
                    nc.vector.tensor_tensor_scan(hh[:, s], av[:, s], uu[:, s], 0.0, ALU.mult, ALU.add)\
                        .then_inc(scan_rdy, 1)
                dve.wait_ge(scan_rdy, HT * (r + 1))
                dve.wait_ge(sg_rdy, r + 1)
                stt(yy[:, :], hh[:, :], 0.5, sg[:, :], ALU.mult, ALU.mult).then_inc(y_rdy, 1)
                if not last:
                    split_lo(S_RV, r + 1, GCHUNK)
                dve.wait_ge(yhi_rdy, r + 1)
                y_hi, y_lo = (xchi, xclo) if last else (yhi, ylo)
                tt(y_lo[:, :], yy[:, :], f(y_hi)[:, :], ALU.subtract).then_inc(ylo_rdy, 1)
                if last:
                    split_lo(S_GK, r + 1)

            round1(0, first=True)
            with dve.Fori(1, NR - 1) as r:
                round1(r)
            round1(NR - 1, last=True)

            def residual(c, n):
                if c < 3:
                    dve.wait_ge(out_done, 3 * n + c + 1)
                else:
                    dve.wait_ge(*((used[S_XQ], 2 * NR + 1) if n else (used[S_O2], 1)))
                s = slice(c * 2 * T, (c + 1) * 2 * T)
                tt(xt[:, s], A[c][:, :], xt[:, s], ALU.add).then_inc(x1_rdy, 1)

            for c in range(5):
                if c < 4:
                    residual(c, 0)
                if c > 0:
                    for k in (2 * c - 2, 2 * c - 1):
                        dve.wait_ge(x1_rdy, c)
                        h_low(k, g_at, 1)
            inverse_rms(1)

            def silu_out(r):
                dve.wait_ge(o_done, r + 1)
                stt(yy[:, :], W[1][:, :], 0.5, sg[:, :], ALU.mult, ALU.mult).then_inc(y_rdy, 1)
                dve.wait_ge(yhi_rdy, NR + r + 1)
                tt(ylo[:, :], yy[:, :], f(yhi)[:, :], ALU.subtract).then_inc(ylo_rdy, 1)

            qk4 = qk[:, :].rearrange("p (t g d) -> p t g d", t=TT, g=4)
            x1v, x2v = qk4[:, :, :, 0:HALF], qk4[:, :, :, HALF:ROT]
            rt5 = rt[:, :].rearrange("p (i t g d) -> p i t g d", i=4, t=TT, g=4)

            def table(t):
                return t.rearrange("p (t a d) -> p t a d", t=TT, a=1).to_broadcast([P, TT, 4, HALF])

            def round2(r, first=False, last=False):
                n = r + NR
                split_lo(S_RV, n)
                if not first:
                    silu_out(r - 1)
                split_lo(S_OG, n - 1)
                dve.wait_ge(q_rdy, r + 1)
                dve.wait_ge(k_rdy, r + 1)
                for i, (a, b) in enumerate(((x1v, cos_t), (x2v, sin_t), (x2v, cos_t), (x1v, sin_t))):
                    tt(rt5[:, i, :, :, :], a, table(b), ALU.mult).then_inc(rope_m, 1)
                dve.wait_ge(rope_m, 4 * r + 4)
                tt(x1v, rt5[:, 0, :, :, :], rt5[:, 1, :, :, :], ALU.subtract)
                tt(x2v, rt5[:, 2, :, :, :], rt5[:, 3, :, :, :], ALU.add).then_inc(rope_rdy, 1)
                if not first:
                    split_lo(S_O2, r)
                dve.wait_ge(t_done, r + 1)
                nc.vector.tensor_copy(kT[:, :], W[1][:, :]).then_inc(kT_rdy, 1)
                split_lo(S_XQ, n + 1)
                if first:
                    dve.wait_ge(rb_rdy, 2)
                dve.wait_ge(used[S_OG], n)
                normalise(gs, W[2]).then_inc(gn_rdy, 1)
                for h, b in ((0, 3), (1, 0)):
                    dve.wait_ge(s_done, 2 * r + h + 1)
                    dia = W[b][:, :].rearrange("p (n m) -> p n m", n=2)[:, :, 0:P]
                    tt(dia, dia, mask.rearrange("p (a m) -> p a m", a=1).to_broadcast([P, 2, P]), ALU.add)\
                        .then_inc(masked, 1)
                    dve.wait_ge(masked, 2 * r + h + 1)
                    nc.vector.reduce_max(mx[:, h * TT:h * TT + 1], W[b][:, 0:P], AX).then_inc(mx_rdy, 1)
                    nc.vector.reduce_max(mx[:, h * TT + 1:h * TT + 2], W[b][:, P:3 * P], AX).then_inc(mx_rdy, 1)
                    dve.wait_ge(mx_rdy, 4 * r + 2 * h + 2)
                    ts(nb[:, h * TT:(h + 1) * TT], mx[:, h * TT:(h + 1) * TT], -SCALE, None, ALU.mult)\
                        .then_inc(nb_rdy, 1)
                dve.wait_ge(tg_rdy, NR + r + 1)
                dve.wait_ge(gn_rdy, n + 1)
                stt(sg[:, :], tg[:, :], 1.0, gs[:, :], ALU.add, ALU.mult).then_inc(sg_rdy, 1)
                for h in range(HT):
                    dve.wait_ge(exp_rdy, 4 * r + 2 * h + 2)
                    nc.vector.reciprocal(rc[:, h * TT:(h + 1) * TT], rs[:, h * TT:(h + 1) * TT]).then_inc(rc_rdy, 1)
                    dve.wait_ge(rc_rdy, 2 * r + h + 1)
                    for t in range(TT):
                        s = slice(h * 3 * P, h * 3 * P + P) if t == 0 else slice(h * 3 * P + P, (h + 1) * 3 * P)
                        ts(pr[:, s], pr[:, s], rc[:, h * TT + t:h * TT + t + 1], None, ALU.mult).then_inc(pr_rdy, 1)
                if not last:
                    split_lo(S_GK, n + 1)
                dve.wait_ge(pT_done, 2 * r + 2)
                nc.vector.tensor_copy(pT[:, 3 * P:6 * P], W[2][:, 0:3 * P]).then_inc(pT_v, 1)

            round2(0, first=True)
            with dve.Fori(1, NR - 1) as r:
                round2(r)
            round2(NR - 1, last=True)
            silu_out(NR - 1)
            for c in range(4):
                residual(c, 1)
            inverse_rms(2)
            dve.wait_ge(rb_done, 3)
            for k in range(KT):
                s = slice(k * T, (k + 1) * T)
                ins = stt(sq[:, s], xt[:, s], g_fin[:, k:k + 1], W[1][:, 0:T], ALU.mult, ALU.mult)
                if k % 2:
                    ins.then_inc(out_rdy, 1)


def kernel(x, rg_norm, rg_w_in, rg_conv_w, rg_conv_b, rg_w_rgate, rg_b_rgate, rg_w_igate, rg_b_igate, rg_lambda,
           rg_w_out, at_norm, at_w_in, at_w_out, final_norm):
    import concourse.bacc as bacc
    from concourse.bass_utils import run_bass_kernel_spmd

    c = np.ascontiguousarray
    f32 = np.float32

    def chunks(w):
        n = w.shape[1] // CW
        return w.reshape(KT, P, n, CW).transpose(2, 1, 0, 3).reshape(n, P, CHUNK)

    def rows(w):
        return w.reshape(NR, HT, P, D).transpose(0, 2, 1, 3).reshape(NR, P, CHUNK)

    out1, out2 = rows(np.asarray(rg_w_out)[0]), rows(np.asarray(at_w_out)[0])
    w_in, w_at = chunks(np.asarray(rg_w_in)[0]), chunks(np.asarray(at_w_in)[0])
    ri = np.stack([np.asarray(rg_w_rgate)[0], np.asarray(rg_w_igate)[0]], 2)
    ri = ri.reshape(NR, HT, P, 2 * CW).transpose(0, 2, 1, 3).reshape(NR, P, GCHUNK)
    per_channel = np.stack([*np.asarray(rg_conv_w)[0], np.asarray(rg_conv_b)[0], np.asarray(rg_b_rgate)[0].reshape(D),
                            np.asarray(rg_b_igate)[0].reshape(D), np.asarray(rg_lambda)[0]])
    inv_freq = f32(500000.0) ** (-np.arange(0, ROT, 2, dtype=f32) / f32(ROT))
    ang = np.arange(T, dtype=f32)[:, None] * inv_freq[None, :]
    rope = np.stack([np.cos(ang), np.sin(ang)]).astype(f32).reshape(2, TT, P, HALF).transpose(2, 0, 1, 3)
    causal = np.where(np.tril(np.ones((P, P), bool)), f32(0), f32(-3e38)).astype(f32)
    arrays = {
        "x_t": np.asarray(x)[0].T.reshape(KT, P, T).transpose(1, 0, 2).reshape(P, KT * T),
        "w_xq": np.concatenate([w_in[:NR], w_at[:NR], out2[NR - 1:]]),
        "w_gk": np.concatenate([w_in[NR:], w_at[NR:2 * NR]]),
        "w_ri": ri,
        "w_v": w_at[2 * NR:3 * NR],
        "w_og": np.concatenate([out1[:NR - 1], w_at[3 * NR:]]),
        "w_o2": np.concatenate([out1[NR - 1:], out2[:NR - 1]]),
        "consts": per_channel.reshape(NCONST, KT, P).transpose(2, 1, 0).reshape(P, KT * NCONST),
        "gains": np.stack([np.asarray(rg_norm)[0], np.asarray(at_norm)[0], np.asarray(final_norm)])
                   .reshape(3, KT, P).transpose(2, 0, 1).reshape(P, 3 * KT),
        "rope": rope.reshape(P, 2 * TT * HALF),
        "ident_mask": np.concatenate([np.eye(P, dtype=f32), causal], 1),
    }
    arrays = {k: c(v) for k, v in arrays.items()}
    nc = bacc.Bacc("TRN2", target_bir_lowering=False, num_devices=1)
    ins = [nc.dram_tensor(k, v.shape, mybir.dt.from_np(v.dtype), kind="ExternalInput").ap() for k, v in arrays.items()]
    out = nc.dram_tensor("out_t", (P, KT * T), F32, kind="ExternalOutput").ap()
    build(nc, *ins, out)
    r = run_bass_kernel_spmd(nc, [arrays], core_ids=[0])
    o = r.results[0]["out_t"]
    return o.reshape(P, KT, T).transpose(2, 1, 0).reshape(1, T, D)
```

```python
from contextlib import ExitStack

import numpy as np

import concourse.bass as bass
from concourse import mybir
from concourse.alu_op_type import AluOpType as ALU

D = 1024
T = 256
P = 128
KT = D // P
WARM = 20
NPIECE = 4
TT = T // P
NR = 4
CW = D // NR
HT = CW // P
TAPS = 4
ROT = 32
HALF = ROT // 2
RTOP = 2 * ROT - HALF
EPS = 1e-6
SCALE = float(P) ** -0.5
NTERM = 8
NCONST = TAPS + 4
CHUNK = KT * CW
GCHUNK = HT * 2 * CW

S_XQ, S_GK, S_RV, S_OG, S_O2 = range(5)
NSLOT = 5

F32, F32R, BF16 = mybir.dt.float32, mybir.dt.float32r, mybir.dt.bfloat16
ACT = mybir.ActivationFunctionType
AX = mybir.AxisListType.X


def build(nc, x_t, w_xq, w_gk, w_ri, w_v, w_og, w_o2, consts, tables, out_t):
    ctx = ExitStack()
    with ctx:
        def sb(name, cols, dt=F32):
            return ctx.enter_context(nc.sbuf_tensor(name, [P, cols], dt))

        def sem(name):
            return ctx.enter_context(nc.semaphore(name))

        raw = [sb(f"raw{j}", CHUNK) for j in range(NSLOT)]
        whi = [sb(f"whi{j}", CHUNK, F32R) for j in range(NSLOT)]
        wlo = [sb(f"wlo{j}", CHUNK, F32R) for j in range(NSLOT)]
        xt = sb("xt", KT * T)
        hhi, hlo = sb("hhi", KT * T, F32R), sb("hlo", KT * T, F32R)
        sq = sb("sq", KT * T)
        cg = sb("cg", (NCONST + 3) * KT)
        tab = sb("tab", 2 * P + 2 * T)
        ones = sb("ones", P)
        ssum = sb("ssum", T)
        ssum2 = sb("ssum2", T)
        xn, gs = sb("xn", HT * T), sb("gs", HT * T)
        zeros = sb("zeros", 2 * T, BF16)
        warm = sb("warm", 1)
        eps, minus1 = sb("eps", 1), sb("minus1", NR * HT)
        half_b = sb("half_b", NR * HT * 2)
        lam = sb("lam", 6 * NR * HT)
        c4 = sb("c4", NR * HT * 2)
        rinv = sb("rinv", T)
        rtok = sb("rtok", 2 * TT)
        diag = sb("diag", T)
        con_v = sb("con_v", HT * NCONST)
        cb_v = sb("cb_v", HT * 4)
        xc = sb("xc", CW * HT)
        xchi, xclo = sb("xchi", HT * T, F32R), sb("xclo", HT * T, F32R)
        tr, ti, tg = sb("tr", HT * T), sb("ti", HT * T), sb("tg", HT * T)
        av, a2 = sb("av", HT * T), sb("a2", HT * T)
        mv, ix = sb("mv", HT * T), sb("ix", HT * T)
        uu, hh = sb("uu", HT * T), sb("hh", HT * T)
        sg, yy = sb("sg", HT * T), sb("yy", HT * T)
        yhi, ylo = sb("yhi", HT * T, F32R), sb("ylo", HT * T, F32R)
        rot = sb("rot", HT * T)
        vv = ix
        qT, kT = tr, ti
        pr = sb("pr", HT * 3 * P)
        pT = sb("pT", HT * 3 * P)
        mx, nb, rs, rc = (sb(n, HT * TT) for n in ("mx", "nb", "rs", "rc"))

        def psum(name):
            return ctx.enter_context(nc.psum_tensor(name, [P, 2 * T], F32))

        W = [psum(f"work{i}") for i in range(4)]
        A = [psum(f"acc{i}") for i in range(4)]

        def v3(t, n, m, at=0):
            return t[:, at:at + n * m].rearrange("p (n m) -> p n m", n=n)

        def f(t):
            return t.bitcast(F32)

        con, gn = cg[:, 0:NCONST * KT], cg[:, NCONST * KT:]
        idm, rp = tab[:, 0:2 * P], tab[:, 2 * P:]
        g_rg, g_at, g_fin = (gn[:, i * KT:(i + 1) * KT] for i in range(3))
        cos_t, sin_t = (rp[:, i * T:(i + 1) * T] for i in range(2))
        ident, mask = idm[:, 0:P], idm[:, P:2 * P]

        sums_before = (0, KT // 2 - 1, KT // 2 - 1 + KT - 1, KT - 2 + KT - 1)
        raw_in = [sem(f"raw_in{j}") for j in range(NSLOT)]
        x_in = [sem(f"x_in{c}") for c in range(NPIECE)]
        w0_in = [sem(f"w0_in{c}") for c in range(2)]
        hi_rdy = [sem(f"hi_rdy{j}") for j in range(NSLOT)]
        lo_rdy = [sem(f"lo_rdy{j}") for j in range(NSLOT)]
        used = [sem(f"used{j}") for j in range(NSLOT)]
        (c_in, i_in, half_hi, half_lo, diag_rdy, rb_done, rb_rdy, const_rdy, sq_rdy, ss_done, std_rdy, h_hi, h_lo, c4_rdy, ssum_step, gn_rdy, xn_rdy, lam_abs, lam_step, hb_rdy, e_lam,
         zero_done, con_v_rdy, cb_v_rdy, i_done, out_done, xc_init, conv_step, xchi_rdy,
         xclo_rdy, tr_rdy, ti_rdy, tg_rdy, a_rdy, a2_rdy, a2c_rdy, m_rdy, ix_rdy, u_rdy, scan_rdy, sg_rdy, y_rdy,
         yhi_rdy, ylo_rdy, x1_rdy, rtok_rdy, q_rdy, k_rdy, v_rdy, rope_step,
         qT_rdy, kT_rdy, s_done, masked, mx_rdy, nb_rdy, exp_rdy, rc_rdy, pr_rdy, pT_done, pT_a,
         pT_v, o_done, out_w, out_rdy, xg_rdy, ssum2_step, pool_out, pool_waited, tg1_rdy) = (sem(n) for n in (
             "c_in i_in half_hi half_lo diag_rdy rb_done rb_rdy const_rdy sq_rdy ss_done std_rdy h_hi h_lo c4_rdy ssum_step gn_rdy xn_rdy lam_abs lam_step hb_rdy e_lam "
             "zero_done con_v_rdy cb_v_rdy i_done out_done xc_init conv_step xchi_rdy "
             "xclo_rdy tr_rdy ti_rdy tg_rdy a_rdy a2_rdy a2c_rdy m_rdy ix_rdy u_rdy scan_rdy sg_rdy y_rdy "
             "yhi_rdy ylo_rdy x1_rdy rtok_rdy q_rdy k_rdy v_rdy rope_step "
             "qT_rdy kT_rdy s_done masked mx_rdy nb_rdy exp_rdy rc_rdy pr_rdy pT_done pT_a "
             "pT_v o_done out_w out_rdy xg_rdy ssum2_step pool_out pool_waited tg1_rdy").split())

        block = ctx.enter_context(nc.Block())

        @block.sync
        def _(sp):
            def load(j, n, dram, at, words=CHUNK, first=False):
                if not first:
                    sp.wait_ge(hi_rdy[j], n)
                    sp.wait_ge(lo_rdy[j], n)
                sp.dma_start(raw[j][:, 0:words],
                             dram[bass.ds(at, 1), :, :].rearrange("a p c -> p (a c)")).then_inc(raw_in[j], 16)

            for c in range(NPIECE):
                w = slice(c * KT * T // NPIECE, (c + 1) * KT * T // NPIECE)
                sp.dma_start(xt[:, w], x_t[:, w]).then_inc(x_in[c], 16)
                if c % 2:
                    w = slice(c // 2 * CHUNK // 2, (c // 2 + 1) * CHUNK // 2)
                    sp.dma_start(raw[S_XQ][:, w], w_xq[0, :, w]).then_inc(w0_in[c // 2], 16)
            load(S_GK, 0, w_gk, 0, first=True)
            load(S_RV, 0, w_ri, 0, GCHUNK, first=True)
            sp.dma_start(tab[:, :], tables).then_inc(i_in, 16)
            load(S_XQ, 1, w_xq, 1)
            load(S_GK, 1, w_gk, 1)
            load(S_RV, 1, w_ri, 1, GCHUNK)
            load(S_XQ, 2, w_xq, 2)
            load(S_OG, 0, w_og, 0, first=True)
            load(S_O2, 0, w_o2, 0, first=True)
            load(S_XQ, 3, w_xq, 3)
            load(S_GK, 2, w_gk, 2)
            load(S_RV, 2, w_ri, 2, GCHUNK)
            load(S_OG, 1, w_og, 1)
            for r in (2, 3):
                load(S_XQ, r + 2, w_xq, r + 2)
                load(S_RV, r + 1, *((w_ri, r + 1, GCHUNK) if r < NR - 1 else (w_v, 0)))
                load(S_GK, r + 1, w_gk, r + 1)
                load(S_OG, r, w_og, r)
            load(S_O2, 1, w_o2, 1)
            load(S_GK, NR + 1, w_gk, NR + 1)
            load(S_RV, NR + 1, w_v, 1)
            for r in range(1, NR):
                load(S_OG, NR + r - 1, w_og, NR + r - 1)
                if r > 1:
                    load(S_O2, r, w_o2, r)
                load(S_XQ, NR + 1 + r, w_xq, NR + 1 + r)
                if r < NR - 1:
                    load(S_GK, NR + 1 + r, w_gk, NR + 1 + r)
                    load(S_RV, NR + 1 + r, w_v, 1 + r)
            for c in range(4):
                sp.wait_ge(*((out_rdy, c + 1) if c < 3 else (pool_out, 1)))
                sp.dma_start(out_t[:, c * 2 * T:(c + 1) * 2 * T], sq[:, c * 2 * T:(c + 1) * 2 * T]).then_inc(out_w, 16)
            sp.wait_ge(out_w, 4 * 16)

        @block.gpsimd
        def _(pool):
            pool.memset(zeros[:, :], 0.0).then_inc(const_rdy, 1)
            pool.memset(ones[:, :], 1.0).then_inc(const_rdy, 1)
            pool.memset(eps[:, :], EPS).then_inc(const_rdy, 1)
            pool.memset(minus1[:, :], -1.0).then_inc(const_rdy, 1)
            pool.memset(rot[:, :], 0.0).then_inc(const_rdy, 1)
            ts, tt = pool.tensor_scalar, pool.tensor_tensor
            pool.wait_ge(c_in, 16)
            L8 = NR * HT
            con3 = v3(con, L8, NCONST)
            lam_in = con3[:, :, NCONST - 1]
            L = [lam[:, i * L8:(i + 1) * L8] for i in range(6)]
            steps = 0

            def chain(ins):
                nonlocal steps
                steps += 1
                ins.then_inc(lam_step, 1)
                pool.wait_ge(lam_step, steps)

            ts(v3(half_b, L8, 2), con3[:, :, TAPS + 1:TAPS + 3], 0.5, None, ALU.mult).then_inc(hb_rdy, 1)
            chain(ts(L[5], lam_in, 0.0, None, ALU.min))
            chain(ts(L[2], lam_in, 0.0, None, ALU.max))
            tt(L[0], L[5], L[2], ALU.subtract).then_inc(lam_abs, 1)

            def log_sigmoid():
                pool.wait_ge(e_lam, 1)
                e = L[1]
                chain(ts(L[2], e, 2.0, None, ALU.add))
                chain(tt(L[3], L[2], minus1[:, :], ALU.pow))
                chain(tt(L[2], e, L[3], ALU.mult))
                chain(tt(L[3], L[2], L[2], ALU.mult))
                chain(ts(L[4], L[3], 1.0 / (2 * NTERM + 1), 1.0 / (2 * NTERM - 1), ALU.mult, ALU.add))
                for i in range(NTERM - 2, -1, -1):
                    chain(tt(L[4], L[4], L[3], ALU.mult))
                    chain(ts(L[4], L[4], 1.0 / (2 * i + 1), None, ALU.add))
                chain(tt(L[4], L[4], L[2], ALU.mult))
                chain(ts(L[4], L[4], -2.0, None, ALU.mult))
                chain(tt(L[4], L[4], L[5], ALU.add))
                c43 = v3(c4, L8, 2)
                ts(c43[:, :, 0], L[4], 4.0, None, ALU.mult).then_inc(c4_rdy, 1)
                ts(c43[:, :, 1], L[4], 8.0, None, ALU.mult).then_inc(c4_rdy, 1)

            log_sigmoid()
            def sum_tiles(n, tiles=KT):
                for k in range(1, tiles):
                    pool.wait_ge(sq_rdy, n * NPIECE + k // 2 + 1)
                    if k == 1 and n:
                        pool.wait_ge(ss_done, n)
                    if k > 1:
                        pool.wait_ge(ssum_step, sums_before[n] + k - 1)
                    a = sq[:, 0:T] if k == 1 else ssum[:, :]
                    tt(ssum[:, :], a, sq[:, k * T:(k + 1) * T], ALU.add).then_inc(ssum_step, 1)

            def waited():
                pool.sem_inc(pool_waited, 1)

            def conv_start(r):
                pool.wait_ge(con_v_rdy, r + 1)
                pool.wait_ge(xn_rdy, r + 1)
                waited()
                for m in range(HT):
                    c0 = m * NCONST
                    ts(xc[:, m * T:(m + 1) * T], xn[:, m * T:(m + 1) * T], con_v[:, c0 + TAPS - 1:c0 + TAPS],
                       con_v[:, c0 + TAPS:c0 + TAPS + 1], ALU.mult, ALU.add).then_inc(xc_init, 1)

            def split_lo(j, n, words=CHUNK):
                pool.wait_ge(hi_rdy[j], n + 1)
                tt(wlo[j][:, 0:words], raw[j][:, 0:words], f(whi[j])[:, 0:words], ALU.subtract).then_inc(lo_rdy[j], 1)

            def round1(r, first=False):
                pool.wait_ge(ix_rdy, r + 1)
                conv_start(r + 1)
                split_lo(S_RV, r + 1, GCHUNK)
                pool.wait_ge(tg_rdy, r + 1)
                waited()
                ts(tg[:, :], tg[:, :], 1.0, 1.0, ALU.mult, ALU.add).then_inc(tg1_rdy, 1)
                if not first:
                    pool.wait_ge(y_rdy, r)
                pool.wait_ge(tg1_rdy, r + 1)
                tt(sg[:, :], tg[:, :], gs[:, :], ALU.mult).then_inc(sg_rdy, 1)

            sum_tiles(0, KT // 2)
            conv_start(0)
            split_lo(S_GK, 1)
            round1(0, first=True)
            pool.wait_ge(raw_in[S_O2], 16)
            pool.tensor_copy(whi[S_O2][:, :], raw[S_O2][:, :]).then_inc(hi_rdy[S_O2], 1)
            with pool.Fori(1, NR - 1) as r:
                round1(r)
            split_lo(S_O2, 0)
            sum_tiles(1)
            split_lo(S_OG, NR - 1)
            split_lo(S_XQ, NR + 1)
            with pool.Fori(1, NR) as r:
                split_lo(S_OG, NR + r - 1)
            sum_tiles(2, KT // 2)
            pool.wait_ge(xg_rdy, NPIECE)
            pool.wait_ge(rb_rdy, 3)
            s = slice((NPIECE - 1) * 2 * T, NPIECE * 2 * T)
            tt(v3(sq, 2, T, s.start), v3(xt, 2, T, s.start),
               rinv[:, :].rearrange("p (a t) -> p a t", a=1).to_broadcast([P, 2, T]), ALU.mult).then_inc(pool_out, 1)

        @block.tensor
        def _(pe):
            def mm(o, w, x, start=False, stop=False):
                return pe.matmul(o, w, x, start=start, stop=stop, skip_group_check=True)

            def split3(o, ahi, alo, bhi, blo, start, stop):
                mm(o, ahi, bhi, start=start)
                mm(o, ahi, blo)
                return mm(o, alo, bhi, stop=stop)

            def chunk_ready(j, n):
                pe.wait_ge(hi_rdy[j], n + 1)
                pe.wait_ge(lo_rdy[j], n + 1)

            def project(j, n, bank, wait_h=0, between={}, halves=None):
                if halves is None:
                    chunk_ready(j, n)
                for k in range(KT):
                    if k in between:
                        between[k]()
                    if halves is not None and k % (KT // 2) == 0:
                        pe.wait_ge(half_hi, halves + 2 * k // KT + 1)
                        pe.wait_ge(half_lo, halves + 2 * k // KT + 1)
                    if wait_h:
                        pe.wait_ge(h_hi, (wait_h - 1) * KT + k + 1)
                        pe.wait_ge(h_lo, (wait_h - 1) * KT + k + 1)
                    for m in range(HT):
                        w = slice(k * CW + m * P, k * CW + m * P + P)
                        h = slice(k * T, (k + 1) * T)
                        last = split3(bank[:, m * T:(m + 1) * T], whi[j][:, w], wlo[j][:, w], hhi[:, h], hlo[:, h],
                                      k == 0 and m == 0, k == KT - 1)
                last.then_inc(used[j], 1)

            def project_tok(j, n, bank):
                chunk_ready(j, n)
                for k in range(KT):
                    for t in range(TT):
                        w = slice(k * CW, (k + 1) * CW)
                        h = slice(k * T + t * P, k * T + t * P + P)
                        last = split3(bank[:, t * CW:(t + 1) * CW], hhi[:, h], hlo[:, h], whi[j][:, w], wlo[j][:, w],
                                      k == 0 and t == 0, k == KT - 1)
                last.then_inc(used[j], 1)

            def clear_acc():
                for a in A:
                    last = mm(a[:, :], zeros[:, 0:P], zeros[:, :], start=True)
                last.then_inc(zero_done, 1)

            def project_out(j, n, yn, last_of_layer=False, y_hi=yhi, y_lo=ylo, between={}):
                chunk_ready(j, n)
                pe.wait_ge(yhi_rdy, yn + 1)
                pe.wait_ge(ylo_rdy, yn + 1)
                for c in range(KT):
                    if c in between:
                        between[c]()
                    for k in range(HT):
                        w = slice(k * D + c * P, k * D + c * P + P)
                        y = slice(k * T, (k + 1) * T)
                        last = split3(A[c // 2][:, (c % 2) * T:(c % 2 + 1) * T], whi[j][:, w], wlo[j][:, w],
                                      y_hi[:, y], y_lo[:, y], False, last_of_layer and k == HT - 1)
                    if last_of_layer and c % 2 == 1 and c < KT - 1:
                        last.then_inc(out_done, 1)
                last.then_inc(used[j], 1)

            def sum_squares(n, bank, parts):
                pe.wait_ge(ssum_step, sums_before[n + 1])
                if len(parts) > 1:
                    pe.wait_ge(ssum2_step, KT // 2 - 1)
                for a in parts:
                    for t in range(TT):
                        last = mm(bank[:, t:t + 1], a[:, t * P:(t + 1) * P], ones[:, 0:1],
                                  start=a is ssum and t == 0, stop=a is parts[-1])
                last.then_inc(ss_done, 1)

            def sum_last_squares():
                for k in (*range(KT // 2, KT - 2), None, KT - 2, KT - 1):
                    if k is None:
                        pe.wait_ge(ssum_step, sums_before[3])
                    elif k % 2 == 0:
                        pe.wait_ge(sq_rdy, 2 * NPIECE + k // 2 + 1)
                    for t in range(TT):
                        a, at = (ssum, 0) if k is None else (sq, k * T)
                        last = mm(W[1][:, t:t + 1], a[:, at + t * P:at + (t + 1) * P], ones[:, 0:1],
                                  start=k == KT // 2 and t == 0, stop=k == KT - 1)
                last.then_inc(ss_done, 1)

            def broadcast_rms(n, bank):
                pe.wait_ge(diag_rdy, n + 1)
                mm(bank[:, 0:T], ones[:, :], diag[:, :], start=True, stop=True).then_inc(rb_done, 1)

            pe.wait_ge(const_rdy, 1)
            for i in range(WARM):
                mm(W[3][:, :], zeros[:, 0:P], zeros[:, :], start=True, stop=True)

            def gates(r, first=False):
                chunk_ready(S_RV, r)
                pe.wait_ge(xchi_rdy, r + 1)
                pe.wait_ge(xclo_rdy, r + 1)
                if first:
                    pe.wait_ge(rb_rdy, 1)
                else:
                    pe.wait_ge(tr_rdy, r)
                    pe.wait_ge(ti_rdy, r)
                for g in (1, 0):
                    for m in range(HT):
                        for k in range(HT):
                            w = slice(k * 2 * CW + g * CW + m * P, k * 2 * CW + g * CW + m * P + P)
                            x = slice(k * T, (k + 1) * T)
                            last = split3(W[2 + g][:, m * T:(m + 1) * T], whi[S_RV][:, w], wlo[S_RV][:, w],
                                          xchi[:, x], xclo[:, x], m == 0 and k == 0, k == HT - 1)
                    last.then_inc(i_done if g else used[S_RV], 1)

            def next_branch(r):
                pe.wait_ge(xn_rdy, r)
                project(S_XQ, r, W[0])

            def this_gate(r):
                pe.wait_ge(gn_rdy, r)
                project(S_GK, r, W[1])

            project(S_XQ, 0, W[0], wait_h=1, halves=0)
            project(S_GK, 0, W[1], halves=2, between={5: lambda: sum_squares(0, W[3], (ssum, ssum2))})
            broadcast_rms(0, W[3])
            project(S_XQ, 1, A[3], halves=4)
            gates(0, first=True)
            pe.wait_ge(xn_rdy, 2)
            clear_acc()
            with pe.Fori(1, NR - 1) as r:
                next_branch(r + 1)
                this_gate(r)
                gates(r)
                project_out(S_OG, r - 1, r - 1)
            gates(NR - 1)
            this_gate(NR - 1)
            project_out(S_OG, NR - 2, NR - 2)
            project_out(S_O2, 0, NR - 1, last_of_layer=True, y_hi=xchi, y_lo=xclo)

            def pv(r):
                pe.wait_ge(pT_a, r + 1)
                pe.wait_ge(pT_v, r + 1)
                for h in range(HT):
                    mm(W[1][:, h * T:(h + 1) * T], vv[:, h * P:(h + 1) * P], pT[:, h * 3 * P:h * 3 * P + T], start=True)
                    last = mm(W[1][:, h * T + P:(h + 1) * T], vv[:, CW + h * P:CW + (h + 1) * P],
                              pT[:, h * 3 * P + T:(h + 1) * 3 * P], stop=True)
                last.then_inc(o_done, 1)

            def scores(r):
                pe.wait_ge(qT_rdy, r + 1)
                pe.wait_ge(kT_rdy, r + 1)
                pe.wait_ge(v_rdy, r + 1)
                for h, b in ((0, 3), (1, 0)):
                    mm(W[b][:, 0:P], qT[:, h * T:h * T + P], kT[:, h * T:h * T + P], start=True, stop=True)
                    mm(W[b][:, P:3 * P], qT[:, h * T + P:(h + 1) * T], kT[:, h * T:(h + 1) * T],
                       start=True, stop=True).then_inc(s_done, 1)

            def key(r):
                pe.wait_ge(gn_rdy, r + NR)
                project(S_GK, r + NR, W[2])

            def attend(r, first=False):
                n = r + NR
                if not first:
                    pe.wait_ge(pT_v, r)
                project_tok(S_RV, n, W[3])
                pe.wait_ge(k_rdy, r + 1)
                project(S_OG, n - 1, W[2], between={2: lambda: scores(r)})
                if first:
                    pe.wait_ge(rb_rdy, 2)
                else:
                    pe.wait_ge(y_rdy, r + NR)
                for h, b in ((0, 1), (1, 3)):
                    pe.wait_ge(pr_rdy, 4 * r + 2 * h + 2)
                    for i in range(3):
                        s = slice((h * 3 + i) * P, (h * 3 + i + 1) * P)
                        last = pe.transpose(W[b][:, i * P:(i + 1) * P], pr[:, s], ident)
                    last.then_inc(pT_done, 1)

            def next_query(r):
                pe.wait_ge(exp_rdy, 4 * r)
                project(S_XQ, r + NR, W[0])

            pe.wait_ge(xn_rdy, NR)
            project(S_XQ, NR, W[0], wait_h=2)
            pe.wait_ge(gn_rdy, NR)
            pe.wait_ge(tr_rdy, NR)
            project(S_GK, NR, W[2], between={2: lambda: sum_squares(1, W[1], (ssum,)), 5: lambda: broadcast_rms(1, W[1])})
            clear_acc()
            pe.wait_ge(ti_rdy, NR)
            attend(0, first=True)
            next_query(1)
            pv(0)
            with pe.Fori(1, NR - 1) as r:
                key(r)
                attend(r)
                project_out(S_O2, r, NR + r - 1, between={KT // 2: lambda: pv(r)})
                next_query(r + 1)
            key(NR - 1)
            attend(NR - 1)
            project_out(S_O2, NR - 1, 2 * NR - 2, between={KT // 2: lambda: pv(NR - 1)})
            project_out(S_XQ, 2 * NR, 2 * NR - 1, last_of_layer=True, y_hi=xchi, y_lo=xclo)
            pe.wait_ge(y_rdy, 2 * NR)
            sum_last_squares()
            broadcast_rms(2, W[1])

        @block.scalar
        def _(act):
            def split_hi(j, n, words=CHUNK, slot_free=False):
                act.wait_ge(raw_in[j], 16 * n if j == S_XQ else 16 * n + 16)
                if not slot_free:
                    act.wait_ge(used[j], n)
                nc.scalar.activation(whi[j][:, 0:words], raw[j][:, 0:words], ACT.Copy).then_inc(hi_rdy[j], 1)

            act.dma_start(cg[:, :], consts).then_inc(c_in, 16)
            act.wait_ge(const_rdy, 3)
            nc.scalar.activation(warm[:, :], eps[:, :], ACT.Exp)
            L8 = NR * HT

            act.wait_ge(c_in, 16)

            def h_high(k, gain):
                nc.scalar.activation(hhi[:, k * T:(k + 1) * T], xt[:, k * T:(k + 1) * T], ACT.Copy,
                                     scale=gain[:, k:k + 1]).then_inc(h_hi, 1)

            def squares(c):
                s = slice(c * KT * T // NPIECE, (c + 1) * KT * T // NPIECE)
                nc.scalar.activation(sq[:, s], xt[:, s], ACT.Square).then_inc(sq_rdy, 1)

            def half_high(j, c):
                w = slice(c * CHUNK // 2, (c + 1) * CHUNK // 2)
                nc.scalar.activation(whi[j][:, w], raw[j][:, w], ACT.Copy).then_inc(half_hi, 1)

            def halves_high(j, before, between=None):
                half_high(j, 0)
                if between:
                    between()
                half_high(j, 1)
                act.wait_ge(half_hi, before + 2)
                act.sem_inc(hi_rdy[j], 1)

            for c in range(NPIECE):
                act.wait_ge(x_in[c], 16)
                h_high(2 * c, g_rg)
                h_high(2 * c + 1, g_rg)
                if c == 1:
                    act.wait_ge(lam_abs, 1)
                    nc.scalar.activation(lam[:, L8:2 * L8], lam[:, 0:L8], ACT.Exp).then_inc(e_lam, 1)
                if c % 2:
                    act.wait_ge(w0_in[c // 2], 16)
                    half_high(S_XQ, c // 2)
            act.wait_ge(half_hi, 2)
            act.sem_inc(hi_rdy[S_XQ], 1)
            squares(0)
            nc.scalar.activation(warm[:, :], eps[:, :], ACT.Sqrt)
            act.wait_ge(raw_in[S_GK], 16)
            halves_high(S_GK, 2)
            for c in range(1, NPIECE):
                squares(c)
            split_hi(S_RV, 0, GCHUNK, slot_free=True)
            act.wait_ge(raw_in[S_XQ], 16)
            act.wait_ge(used[S_XQ], 1)
            def rms(n, bank):
                act.wait_ge(ss_done, n + 1)
                nc.scalar.activation(rtok[:, 0:TT], bank[:, 0:TT], ACT.Sqrt, bias=eps[:, :], scale=1.0 / D)\
                    .then_inc(std_rdy, 1)

            def keep_rms(n, bank):
                act.wait_ge(rb_done, n + 1)
                nc.scalar.activation(rinv[:, :], bank[:, 0:T], ACT.Copy).then_inc(rb_rdy, 1)

            halves_high(S_XQ, 4, between=lambda: rms(0, W[3]))
            keep_rms(0, W[3])
            split_hi(S_GK, 1)
            split_hi(S_XQ, 2)
            nc.scalar.activation(warm[:, :], eps[:, :], ACT.Exp)

            def round1(r, first=False, last=False):
                def gate_tanh():
                    act.wait_ge(gn_rdy, r + 1)
                    if not first:
                        act.wait_ge(sg_rdy, r)
                    nc.scalar.activation(tg[:, :], gs[:, :], ACT.Tanh, scale=0.5).then_inc(tg_rdy, 1)

                if not first and not last:
                    split_hi(S_XQ, r + 2)
                act.wait_ge(cb_v_rdy, 2 * r + 2)
                for g, t, rdy in ((1, ti, ti_rdy), (0, tr, tr_rdy)):
                    act.wait_ge(i_done if g else used[S_RV], r + 1)
                    if g == 1 and not first:
                        act.wait_ge(ix_rdy, r)
                    for m in range(HT):
                        ins = nc.scalar.activation(t[:, m * T:(m + 1) * T], W[2 + g][:, m * T:(m + 1) * T], ACT.Tanh,
                                                   bias=cb_v[:, m * 2 + g:m * 2 + g + 1], scale=0.5)
                    ins.then_inc(rdy, 1)
                if not last:
                    split_hi(S_RV, r + 1, GCHUNK)
                act.wait_ge(tr_rdy, r + 1)
                if not first:
                    act.wait_ge(scan_rdy, HT * r)
                    act.wait_ge(m_rdy, r)
                for i, (dst, rdy) in enumerate(((a2, a2_rdy), (av, a_rdy))):
                    for m in range(HT):
                        c = cb_v[:, HT * 2 + m * 2 + 1 - i:HT * 2 + m * 2 + 2 - i]
                        nc.scalar.activation(dst[:, m * T:(m + 1) * T], tr[:, m * T:(m + 1) * T], ACT.Exp,
                                             bias=c, scale=c).then_inc(rdy, 1)
                if not last:
                    gate_tanh()
                    if not first:
                        split_hi(S_GK, r + 1)
                act.wait_ge(a2c_rdy, r + 1)
                if not first:
                    act.wait_ge(u_rdy, r)
                nc.scalar.activation(mv[:, :], a2[:, :], ACT.Sqrt, bias=1.0, scale=-1.0).then_inc(m_rdy, 1)
                if last:
                    gate_tanh()
                else:
                    split_hi(S_OG, r, slot_free=first)
                if not last:
                    nc.scalar.activation(warm[:, :], eps[:, :], ACT.Exp)
                if last:
                    split_hi(S_GK, r + 1)

            round1(0, first=True)
            with act.Fori(1, NR - 1) as r:
                round1(r)
            round1(NR - 1, last=True)

            act.wait_ge(used[S_GK], NR)
            for c in range(NPIECE):
                act.wait_ge(x1_rdy, c + 1)
                h_high(2 * c, g_at)
                h_high(2 * c + 1, g_at)
                squares(c)
            rms(1, W[1])
            split_hi(S_RV, NR)
            act.wait_ge(rtok_rdy, 2)

            def token_scaled(dst, bank, rdy):
                for t in range(TT):
                    ins = nc.scalar.activation(dst(t), bank[:, t * CW:(t + 1) * CW], ACT.Copy,
                                               scale=rtok[:, TT + t:TT + t + 1])
                ins.then_inc(rdy, 1)

            def round2(r, first=False, last=False):
                n = r + NR
                split_hi(S_OG, n - 1)
                if first:
                    keep_rms(1, W[1])
                if not first:
                    split_hi(S_O2, r)
                act.wait_ge(used[S_RV], n + 1)
                if not first:
                    act.wait_ge(o_done, r)
                token_scaled(lambda t: vv[:, t * CW:(t + 1) * CW], W[3], v_rdy)
                split_hi(S_XQ, n + 1)
                for h, b in ((0, 3), (1, 0)):
                    act.wait_ge(nb_rdy, 2 * r + h + 1)
                    if not first:
                        act.wait_ge(pT_done, 2 * r)
                        act.wait_ge(rc_rdy, 2 * r)
                    for t in range(TT):
                        s = slice(0, P) if t == 0 else slice(P, 3 * P)
                        nc.scalar.activation(pr[:, h * 3 * P + s.start:h * 3 * P + s.stop], W[b][:, s], ACT.Exp,
                                             bias=nb[:, h * TT + t:h * TT + t + 1], scale=SCALE,
                                             accum_out=rs[:, h * TT + t:h * TT + t + 1]).then_inc(exp_rdy, 1)
                act.wait_ge(pT_done, 2 * r + 1)
                nc.scalar.activation(pT[:, 0:3 * P], W[1][:, 0:3 * P], ACT.Copy).then_inc(pT_a, 1)
                act.wait_ge(gn_rdy, n + 1)
                nc.scalar.activation(tg[:, :], gs[:, :], ACT.Tanh, scale=0.5).then_inc(tg_rdy, 1)
                if not last:
                    split_hi(S_GK, n + 1)
                    split_hi(S_RV, n + 1)

            round2(0, first=True)
            with act.Fori(1, NR - 1) as r:
                round2(r)
            round2(NR - 1, last=True)

            nc.scalar.activation(warm[:, :], eps[:, :], ACT.Sqrt)
            for c in range(NPIECE):
                act.wait_ge(x1_rdy, NPIECE + c + 1)
                squares(c)
            rms(2, W[1])
            keep_rms(2, W[1])

        @block.vector
        def _(dve):
            tt, stt, ts = nc.vector.tensor_tensor, nc.vector.scalar_tensor_tensor, nc.vector.tensor_scalar

            def split_lo(j, n, words=CHUNK):
                dve.wait_ge(hi_rdy[j], n + 1)
                tt(wlo[j][:, 0:words], raw[j][:, 0:words], f(whi[j])[:, 0:words], ALU.subtract)\
                    .then_inc(lo_rdy[j], 1)

            dve.wait_ge(c_in, 16)

            def h_low(k, gain, n):
                s = slice(k * T, (k + 1) * T)
                dve.wait_ge(h_hi, n * KT + k + 1)
                stt(hlo[:, s], xt[:, s], gain[:, k:k + 1], f(hhi)[:, s], ALU.mult, ALU.subtract).then_inc(h_lo, 1)

            def half_low(j, c, n):
                w = slice(c * CHUNK // 2, (c + 1) * CHUNK // 2)
                dve.wait_ge(half_hi, n)
                tt(wlo[j][:, w], raw[j][:, w], f(whi[j])[:, w], ALU.subtract).then_inc(half_lo, 1)

            def both_halves(j, n):
                dve.wait_ge(half_lo, n)
                dve.sem_inc(lo_rdy[j], 1)

            for c in range(2):
                for k in range(c * KT // 2, (c + 1) * KT // 2):
                    h_low(k, g_rg, 0)
                half_low(S_XQ, c, c + 1)
            both_halves(S_XQ, 2)
            half_low(S_GK, 0, 3)
            half_low(S_GK, 1, 4)
            both_halves(S_GK, 4)

            def inverse_rms(n):
                dve.wait_ge(std_rdy, n + 1)
                if n:
                    dve.wait_ge(rb_done, n)
                nc.vector.reciprocal(rtok[:, TT:2 * TT], rtok[:, 0:TT]).then_inc(rtok_rdy, 1)
                dve.wait_ge(rtok_rdy, n + 1)
                for t in range(TT):
                    ins = ts(diag[:, t * P:(t + 1) * P], ident, rtok[:, TT + t:TT + t + 1], None, ALU.mult)
                ins.then_inc(diag_rdy, 1)

            dve.wait_ge(i_in, 16)
            for k in range(KT // 2 + 1, KT):
                i = k - KT // 2
                if i > 1:
                    dve.wait_ge(ssum2_step, i - 1)
                dve.wait_ge(sq_rdy, k // 2 + 1)
                a = sq[:, KT // 2 * T:(KT // 2 + 1) * T] if i == 1 else ssum2[:, :]
                tt(ssum2[:, :], a, sq[:, k * T:(k + 1) * T], ALU.add).then_inc(ssum2_step, 1)
            split_lo(S_RV, 0, GCHUNK)
            half_low(S_XQ, 0, 5)
            inverse_rms(0)
            half_low(S_XQ, 1, 6)
            both_halves(S_XQ, 6)

            def normalise(dst, bank):
                return tt(v3(dst, HT, T), v3(bank, HT, T),
                          rinv[:, :].rearrange("p (a t) -> p a t", a=1).to_broadcast([P, HT, T]), ALU.mult)

            def branch(r, bank):
                nc.vector.tensor_copy(con_v[:, :], v3(con, NR, HT * NCONST)[:, bass.ds(r, 1), :]
                                      .rearrange("p a c -> p (a c)")).then_inc(con_v_rdy, 1)
                dve.wait_ge(used[S_XQ], r + 1)
                normalise(xn, bank).then_inc(xn_rdy, 1)

            def gate(r):
                dve.wait_ge(used[S_GK], r + 1)
                normalise(gs, W[1]).then_inc(gn_rdy, 1)

            def conv(r):
                dve.wait_ge(con_v_rdy, r + 1)
                dve.wait_ge(xn_rdy, r + 1)
                for i in range(1, TAPS):
                    for m in range(HT):
                        dve.wait_ge(xc_init, HT * r + m + 1)
                        if i > 1:
                            dve.wait_ge(conv_step, 6 * r + (i - 2) * HT + m + 1)
                        c = m * NCONST + TAPS - 1 - i
                        o = xc[:, m * T + i:(m + 1) * T]
                        stt(o, xn[:, m * T:(m + 1) * T - i], con_v[:, c:c + 1], o, ALU.mult, ALU.add)\
                            .then_inc(conv_step, 1)

            def y_split(n, other):
                y_hi, y_lo = (xchi, xclo) if other else (yhi, ylo)
                dve.wait_ge(y_rdy, n + 1)
                nc.vector.tensor_copy(y_hi[:, :], yy[:, :]).then_inc(yhi_rdy, 1)
                dve.wait_ge(yhi_rdy, n + 1)
                tt(y_lo[:, :], yy[:, :], f(y_hi)[:, :], ALU.subtract).then_inc(ylo_rdy, 1)

            def gate_constants(r):
                for src, at in ((half_b, 0), (c4, HT * 2)):
                    nc.vector.tensor_copy(cb_v[:, at:at + HT * 2], v3(src, NR, HT * 2)[:, bass.ds(r, 1), :]
                                          .rearrange("p a c -> p (a c)")).then_inc(cb_v_rdy, 1)

            def conv_split(r):
                dve.wait_ge(conv_step, 6 * r + 6)
                nc.vector.tensor_copy(xchi[:, :], xc[:, :]).then_inc(xchi_rdy, 1)
                dve.wait_ge(xchi_rdy, r + 1)
                tt(xclo[:, :], xc[:, :], f(xchi)[:, :], ALU.subtract).then_inc(xclo_rdy, 1)

            dve.wait_ge(rb_rdy, 1)
            branch(0, W[0])
            gate(0)
            conv(0)
            conv_split(0)
            dve.wait_ge(hb_rdy, 1)
            dve.wait_ge(c4_rdy, 2)
            gate_constants(0)

            def round1(r, first=False, last=False):
                if not last:
                    branch(r + 1, A[3] if first else W[0])
                    split_lo(S_XQ, r + 2)
                dve.wait_ge(ti_rdy, r + 1)
                if not first:
                    dve.wait_ge(u_rdy, r)
                stt(ix[:, :], ti[:, :], 1.0, xc[:, :], ALU.add, ALU.mult).then_inc(ix_rdy, 1)
                if not first and not last:
                    gate(r)
                if not last:
                    conv(r + 1)
                dve.wait_ge(a2_rdy, HT * (r + 1))
                ts(a2[:, :], a2[:, :], 1.0, None, ALU.min).then_inc(a2c_rdy, 1)
                if last:
                    gate(r)
                else:
                    dve.wait_ge(used[S_RV], r + 1)
                    conv_split(r + 1)
                    if not first:
                        split_lo(S_GK, r + 1)
                dve.wait_ge(m_rdy, r + 1)
                dve.wait_ge(ix_rdy, r + 1)
                stt(uu[:, :], mv[:, :], 0.5, ix[:, :], ALU.mult, ALU.mult).then_inc(u_rdy, 1)
                dve.wait_ge(u_rdy, r + 1)
                dve.wait_ge(a_rdy, HT * (r + 1))
                for m in range(HT):
                    s = slice(m * T, (m + 1) * T)
                    nc.vector.tensor_tensor_scan(hh[:, s], av[:, s], uu[:, s], 0.0, ALU.mult, ALU.add)\
                        .then_inc(scan_rdy, 1)
                if last:
                    dve.wait_ge(tg_rdy, r + 1)
                    dve.wait_ge(gn_rdy, r + 1)
                    stt(sg[:, :], tg[:, :], 1.0, gs[:, :], ALU.add, ALU.mult).then_inc(sg_rdy, 1)
                dve.wait_ge(scan_rdy, HT * (r + 1))
                dve.wait_ge(sg_rdy, r + 1)
                stt(yy[:, :], hh[:, :], 0.5, sg[:, :], ALU.mult, ALU.mult).then_inc(y_rdy, 1)
                if not last:
                    gate_constants(r + 1)
                    split_lo(S_OG, r)
                if not first and not last:
                    dve.wait_ge(used[S_OG], r)
                y_split(r, last)
                if last:
                    split_lo(S_GK, r + 1)

            round1(0, first=True)
            with dve.Fori(1, NR - 1) as r:
                round1(r)
            round1(NR - 1, last=True)

            def residual(c, n):
                if c < 3:
                    dve.wait_ge(out_done, 3 * n + c + 1)
                else:
                    dve.wait_ge(*((used[S_XQ], 2 * NR + 1) if n else (used[S_O2], 1)))
                s = slice(c * 2 * T, (c + 1) * 2 * T)
                tt(xt[:, s], A[c][:, :], xt[:, s], ALU.add).then_inc(x1_rdy, 1)

            for c in range(5):
                if c < 4:
                    residual(c, 0)
                if c > 0:
                    for k in (2 * c - 2, 2 * c - 1):
                        dve.wait_ge(x1_rdy, c)
                        h_low(k, g_at, 1)
            inverse_rms(1)

            def silu_out(r, first=False, last=False):
                dve.wait_ge(o_done, r + 1)
                dve.wait_ge(sg_rdy, NR + r + 1)
                stt(yy[:, :], W[1][:, :], 0.5, sg[:, :], ALU.mult, ALU.mult).then_inc(y_rdy, 1)
                if not first and not last:
                    dve.wait_ge(used[S_O2], r + 1)
                y_split(NR + r, last)

            def on_heads(table, at, n):
                return table[at:at + n, :].rearrange("p (a t) -> p a t", a=1).to_broadcast([n, HT, T])

            def rotate(r, steps, slot, bank, dst, read, rdy):
                dve.wait_ge(used[slot], r + NR + 1)
                normalise(dst, bank).then_inc(read, 1)
                dve.wait_ge(read, r + 1)

                def part(x, at, n):
                    return x[at:at + n, :].rearrange("p (a t) -> p a t", a=HT)

                for src, to in ((0, ROT), (ROT, 0)):
                    tt(part(rot, to, HALF), part(dst, src, HALF), on_heads(sin_t, src, HALF), ALU.mult)\
                        .then_inc(rope_step, 1)
                dve.wait_ge(rope_step, 6 * r + steps + 2)
                tt(part(dst, 0, RTOP), part(dst, 0, RTOP), on_heads(cos_t, 0, RTOP), ALU.mult).then_inc(rope_step, 1)
                dve.wait_ge(rope_step, 6 * r + steps + 3)
                tt(dst[0:RTOP, :], dst[0:RTOP, :], rot[0:RTOP, :], ALU.add).then_inc(rdy, 1)

            def round2(r, first=False, last=False):
                n = r + NR
                if first:
                    split_lo(S_RV, n)
                    dve.wait_ge(rb_rdy, 2)
                    dve.wait_ge(const_rdy, 5)
                rotate(r, 0, S_XQ, W[0], qT, q_rdy, qT_rdy)
                rotate(r, 3, S_GK, W[2], kT, k_rdy, kT_rdy)
                if not first:
                    split_lo(S_O2, r)
                for h, b in ((0, 3), (1, 0)):
                    dve.wait_ge(s_done, 2 * r + h + 1)
                    dia = W[b][:, :].rearrange("p (n m) -> p n m", n=2)[:, :, 0:P]
                    tt(dia, dia, mask.rearrange("p (a m) -> p a m", a=1).to_broadcast([P, 2, P]), ALU.add)\
                        .then_inc(masked, 1)
                    dve.wait_ge(masked, 2 * r + h + 1)
                    nc.vector.reduce_max(mx[:, h * TT:h * TT + 1], W[b][:, 0:P], AX).then_inc(mx_rdy, 1)
                    nc.vector.reduce_max(mx[:, h * TT + 1:h * TT + 2], W[b][:, P:3 * P], AX).then_inc(mx_rdy, 1)
                    dve.wait_ge(mx_rdy, 4 * r + 2 * h + 2)
                    ts(nb[:, h * TT:(h + 1) * TT], mx[:, h * TT:(h + 1) * TT], -SCALE, None, ALU.mult)\
                        .then_inc(nb_rdy, 1)
                for h in range(HT):
                    dve.wait_ge(exp_rdy, 4 * r + 2 * h + 2)
                    nc.vector.reciprocal(rc[:, h * TT:(h + 1) * TT], rs[:, h * TT:(h + 1) * TT]).then_inc(rc_rdy, 1)
                    dve.wait_ge(rc_rdy, 2 * r + h + 1)
                    for t in range(TT):
                        s = slice(h * 3 * P, h * 3 * P + P) if t == 0 else slice(h * 3 * P + P, (h + 1) * 3 * P)
                        ts(pr[:, s], pr[:, s], rc[:, h * TT + t:h * TT + t + 1], None, ALU.mult).then_inc(pr_rdy, 1)
                dve.wait_ge(used[S_OG], n)
                normalise(gs, W[2]).then_inc(gn_rdy, 1)
                dve.wait_ge(pT_done, 2 * r + 2)
                nc.vector.tensor_copy(pT[:, 3 * P:6 * P], W[3][:, 0:3 * P]).then_inc(pT_v, 1)
                if not first:
                    split_lo(S_XQ, n + 1)
                dve.wait_ge(tg_rdy, NR + r + 1)
                dve.wait_ge(gn_rdy, n + 1)
                stt(sg[:, :], tg[:, :], 1.0, gs[:, :], ALU.add, ALU.mult).then_inc(sg_rdy, 1)
                if not last:
                    split_lo(S_GK, n + 1)
                    split_lo(S_RV, n + 1)
                silu_out(r, first, last)

            round2(0, first=True)
            with dve.Fori(1, NR - 1) as r:
                round2(r)
            round2(NR - 1, last=True)
            for c in range(4):
                residual(c, 1)
            for c in range(NPIECE):
                dve.wait_ge(sq_rdy, 2 * NPIECE + c + 1)
                for k in (2 * c, 2 * c + 1):
                    ins = ts(xt[:, k * T:(k + 1) * T], xt[:, k * T:(k + 1) * T], g_fin[:, k:k + 1], None, ALU.mult)
                ins.then_inc(xg_rdy, 1)
            inverse_rms(2)
            dve.wait_ge(rb_rdy, 3)
            for c in range(NPIECE - 1):
                dve.wait_ge(xg_rdy, c + 1)
                tt(v3(sq, 2, T, c * 2 * T), v3(xt, 2, T, c * 2 * T),
                   rinv[:, :].rearrange("p (a t) -> p a t", a=1).to_broadcast([P, 2, T]), ALU.mult).then_inc(out_rdy, 1)


def kernel(x, rg_norm, rg_w_in, rg_conv_w, rg_conv_b, rg_w_rgate, rg_b_rgate, rg_w_igate, rg_b_igate, rg_lambda,
           rg_w_out, at_norm, at_w_in, at_w_out, final_norm):
    import concourse.bacc as bacc
    from concourse.bass_utils import run_bass_kernel_spmd

    c = np.ascontiguousarray
    f32 = np.float32

    def chunks(w):
        n = w.shape[1] // CW
        return w.reshape(KT, P, n, CW).transpose(2, 1, 0, 3).reshape(n, P, CHUNK)

    def rows(w):
        return w.reshape(NR, HT, P, D).transpose(0, 2, 1, 3).reshape(NR, P, CHUNK)

    out1, out2 = rows(np.asarray(rg_w_out)[0]), rows(np.asarray(at_w_out)[0])
    w_in, w_at = chunks(np.asarray(rg_w_in)[0]), chunks(np.asarray(at_w_in)[0])
    qk_heads = (2 * NR, P, KT, HT, P)
    ri = np.stack([np.asarray(rg_w_rgate)[0], np.asarray(rg_w_igate)[0]], 2)
    ri = ri.reshape(NR, HT, P, 2 * CW).transpose(0, 2, 1, 3).reshape(NR, P, GCHUNK)
    per_channel = np.stack([*np.asarray(rg_conv_w)[0], np.asarray(rg_conv_b)[0], np.asarray(rg_b_rgate)[0].reshape(D),
                            np.asarray(rg_b_igate)[0].reshape(D), np.asarray(rg_lambda)[0]])
    inv_freq = f32(500000.0) ** (-np.arange(0, ROT, 2, dtype=f32) / f32(ROT))
    ang = np.arange(T, dtype=f32)[:, None] * inv_freq[None, :]
    cos, sin = np.cos(ang).astype(f32).T, np.sin(ang).astype(f32).T
    rope = np.zeros((P, 2, T), f32)
    rope[HALF:ROT, 0] = 1
    for at, sign in ((0, 1), (ROT, -1)):
        rope[at:at + HALF, 0], rope[at:at + HALF, 1] = cos, sign * sin
    dims = np.r_[0:HALF, ROT:ROT + HALF, HALF:ROT, ROT + HALF:P]
    causal = np.where(np.tril(np.ones((P, P), bool)), f32(0), f32(-3e38)).astype(f32)
    w_at[:2 * NR] = w_at[:2 * NR].reshape(qk_heads)[..., dims].reshape(2 * NR, P, CHUNK)
    arrays = {
        "x_t": np.asarray(x)[0].T.reshape(KT, P, T).transpose(1, 0, 2).reshape(P, KT * T),
        "w_xq": np.concatenate([w_in[:NR], w_at[:NR], out2[NR - 1:]]),
        "w_gk": np.concatenate([w_in[NR:], w_at[NR:2 * NR]]),
        "w_ri": ri,
        "w_v": w_at[2 * NR:3 * NR],
        "w_og": np.concatenate([out1[:NR - 1], w_at[3 * NR:]]),
        "w_o2": np.concatenate([out1[NR - 1:], out2[:NR - 1]]),
        "consts": np.concatenate([
            per_channel.reshape(NCONST, KT, P).transpose(2, 1, 0).reshape(P, KT * NCONST),
            np.stack([np.asarray(rg_norm)[0], np.asarray(at_norm)[0], np.asarray(final_norm)])
              .reshape(3, KT, P).transpose(2, 0, 1).reshape(P, 3 * KT)], 1),
        "tables": np.concatenate([np.eye(P, dtype=f32), causal, rope.reshape(P, 2 * T)], 1),
    }
    arrays = {k: c(v) for k, v in arrays.items()}
    nc = bacc.Bacc("TRN2", target_bir_lowering=False, num_devices=1)
    ins = [nc.dram_tensor(k, v.shape, mybir.dt.from_np(v.dtype), kind="ExternalInput").ap() for k, v in arrays.items()]
    out = nc.dram_tensor("out_t", (P, KT * T), F32, kind="ExternalOutput").ap()
    build(nc, *ins, out)
    r = run_bass_kernel_spmd(nc, [arrays], core_ids=[0])
    o = r.results[0]["out_t"]
    return o.reshape(P, KT, T).transpose(2, 1, 0).reshape(1, T, D)
```
